# Optimizing a Trainium2 kernel written in Bass

```python
import jax, jax.numpy as jnp
from jax import lax
import numpy as np

D_MODEL = 1024
BATCH = 1
SEQ = 256
DEPTH = 2
DEC_BATCH = 8
DEC_SEQ = 1
PAST_LEN = 2048
PAGE_SIZE = 128

MIX_WIDTH = D_MODEL
MLSTM_WIDTH = MIX_WIDTH // 2
POOL_WIDTH = MIX_WIDTH - MLSTM_WIDTH
MLSTM_HEADS = 4
HEAD_DIM = MLSTM_WIDTH // MLSTM_HEADS
MLSTM_CHUNK = 64
POOL_WINDOWS = (2, 4, 8, 16)
POOL_GROUPS = len(POOL_WINDOWS)
POOL_GROUP = POOL_WIDTH // POOL_GROUPS
POOL_BUF = max(POOL_WINDOWS) - 1
PROJ_WIDTH = 4 * MLSTM_WIDTH + POOL_WIDTH + 2 * MLSTM_HEADS
PEER_HEADS = 8
PEER_NKEYS = 128
PEER_EXPERTS = PEER_NKEYS * PEER_NKEYS
PEER_QDIM = 256
PEER_HALF = PEER_QDIM // 2
PEER_TOPK = 16
PEER_BLOCK = 128
PLE_DIM = 256
EPS = 1e-6

kernel_name = "hymba_mlstm_pool_peer_step"

def rmsnorm(x, g):
    xf = x.astype(jnp.float32)
    y = xf * lax.rsqrt(jnp.mean(xf * xf, axis=-1, keepdims=True) + EPS)
    return (y * g.astype(jnp.float32)).astype(x.dtype)

def mlstm_chunk(carry, xs):
    C, n, m = carry
    q, k, v, ig, lf = xs
    L = q.shape[2]
    b = jnp.cumsum(lf, axis=-1)
    causal = jnp.tril(jnp.ones((L, L), dtype=bool))
    dlog = jnp.where(causal, b[..., :, None] - b[..., None, :] + ig[..., None, :], -jnp.inf)
    inter = b + m[..., None]
    m_t = jnp.maximum(jnp.max(dlog, axis=-1), inter)
    s = jnp.einsum('bhtd,bhsd->bhts', q, k) * jnp.exp(dlog - m_t[..., None])
    w_inter = jnp.exp(inter - m_t)
    num = jnp.einsum('bhts,bhsd->bhtd', s, v) + w_inter[..., None] * jnp.einsum('bhtd,bhde->bhte', q, C)
    den = jnp.sum(s, axis=-1) + w_inter * jnp.einsum('bhtd,bhd->bht', q, n)
    h = num / jnp.maximum(jnp.abs(den), jnp.exp(-m_t))[..., None]
    b_last = b[..., -1]
    wlog = b_last[..., None] - b + ig
    m_new = jnp.maximum(b_last + m, jnp.max(wlog, axis=-1))
    decay = jnp.exp(b_last + m - m_new)
    ws = jnp.exp(wlog - m_new[..., None])
    C_new = decay[..., None, None] * C + jnp.einsum('bhs,bhsd,bhse->bhde', ws, k, v)
    n_new = decay[..., None] * n + jnp.einsum('bhs,bhsd->bhd', ws, k)
    return (C_new, n_new, m_new), h

def mlstm_mixer(q, k, v, ig, lf, C, n, m):
    q, k, v = (jnp.swapaxes(a, 1, 2) for a in (q, k, v))
    ig, lf = (jnp.swapaxes(a, 1, 2) for a in (ig, lf))
    B, H, T, d = q.shape
    carry = (C.astype(jnp.float32), n.astype(jnp.float32), m.astype(jnp.float32))
    if T > MLSTM_CHUNK and T % MLSTM_CHUNK == 0:
        nc = T // MLSTM_CHUNK

        def to_chunks(a):
            a = a.reshape(a.shape[:2] + (nc, MLSTM_CHUNK) + a.shape[3:])
            return jnp.moveaxis(a, 2, 0)

        carry, h = lax.scan(mlstm_chunk, carry, tuple(to_chunks(a) for a in (q, k, v, ig, lf)))
        h = jnp.moveaxis(h, 0, 2).reshape(B, H, T, d)
    else:
        carry, h = mlstm_chunk(carry, (q, k, v, ig, lf))
    return jnp.swapaxes(h, 1, 2), carry

def pool_mixer(u, buf, start, w_pool, pool_scale):
    B, T, P = u.shape
    ext = jnp.concatenate([buf.astype(jnp.float32), u], axis=1)
    cs = jnp.concatenate([jnp.zeros((B, 1, P), jnp.float32), jnp.cumsum(ext, axis=1)], axis=1)
    pos = start + jnp.arange(T)
    outs = []
    for g, w in enumerate(POOL_WINDOWS):
        lo_c, hi_c = g * POOL_GROUP, (g + 1) * POOL_GROUP
        hi = cs[:, POOL_BUF + 1:POOL_BUF + 1 + T, lo_c:hi_c]
        lo = cs[:, POOL_BUF + 1 - w:POOL_BUF + 1 - w + T, lo_c:hi_c]
        cnt = jnp.minimum(pos + 1, w).astype(jnp.float32)[None, :, None]
        outs.append((hi - lo) / cnt - u[:, :, lo_c:hi_c])
    r = jnp.stack(outs, axis=2)
    z = jnp.einsum('btgc,gcd->btgd', r, w_pool.astype(jnp.float32)).reshape(B, T, P)
    z = z * pool_scale.astype(jnp.float32)
    return z, ext[:, -POOL_BUF:]

def peer_ffn(xn, wq, sub_keys, u_tab, v_tab):
    B, T, D = xn.shape
    flat = xn.reshape(B * T, D)
    ntok = B * T
    pad = (-ntok) % PEER_BLOCK
    flat = jnp.pad(flat, ((0, pad), (0, 0)))
    blocks = flat.reshape(-1, PEER_BLOCK, D)
    keys = sub_keys.astype(jnp.float32)

    def block_fn(xb):
        q = (xb @ wq).astype(jnp.float32).reshape(PEER_BLOCK, PEER_HEADS, 2, PEER_HALF)
        s = jnp.einsum('thcd,chkd->thck', q, keys)
        sv, si = lax.top_k(s, PEER_TOPK)
        cand = (sv[:, :, 0, :, None] + sv[:, :, 1, None, :]).reshape(PEER_BLOCK, PEER_HEADS, PEER_TOPK * PEER_TOPK)
        cidx = (si[:, :, 0, :, None] * PEER_NKEYS + si[:, :, 1, None, :]).reshape(PEER_BLOCK, PEER_HEADS, PEER_TOPK * PEER_TOPK)
        top, sel = lax.top_k(cand, PEER_TOPK)
        eidx = jnp.take_along_axis(cidx, sel, axis=-1)
        gate = jax.nn.softmax(top, axis=-1)
        ue = u_tab[eidx]
        act = jax.nn.gelu(jnp.einsum('td,thkd->thk', xb, ue).astype(jnp.float32))
        ve = v_tab[eidx]
        return jnp.einsum('thk,thkd->td', (gate * act).astype(xb.dtype), ve)

    out = lax.map(block_fn, blocks).reshape(-1, D)[:ntok]
    return out.reshape(B, T, D)

def layer(x, p, C, n, m, buf, start, w_in, b_gate, mlstm_norm, w_pool, pool_scale, w_out,
          norm1, norm2, peer_wq, peer_keys, peer_u, peer_v, w_ple, w_gate):
    B, T, _ = x.shape
    h = rmsnorm(x, norm1)
    proj = h @ w_in
    W = MLSTM_WIDTH
    q = proj[..., 0:W].astype(jnp.float32).reshape(B, T, MLSTM_HEADS, HEAD_DIM)
    k = proj[..., W:2 * W].astype(jnp.float32).reshape(B, T, MLSTM_HEADS, HEAD_DIM) * (HEAD_DIM ** -0.5)
    v = proj[..., 2 * W:3 * W].astype(jnp.float32).reshape(B, T, MLSTM_HEADS, HEAD_DIM)
    o = jax.nn.sigmoid(proj[..., 3 * W:4 * W].astype(jnp.float32))
    u_pool = proj[..., 4 * W:4 * W + POOL_WIDTH].astype(jnp.float32)
    gates = proj[..., 4 * W + POOL_WIDTH:].astype(jnp.float32) + b_gate.astype(jnp.float32)
    ig = gates[..., :MLSTM_HEADS]
    lf = jax.nn.log_sigmoid(gates[..., MLSTM_HEADS:])
    hm, (C_new, n_new, m_new) = mlstm_mixer(q, k, v, ig, lf, C, n, m)
    hm = hm * lax.rsqrt(jnp.mean(hm * hm, axis=-1, keepdims=True) + EPS)
    hm = hm.reshape(B, T, MLSTM_WIDTH) * mlstm_norm.astype(jnp.float32) * o
    zp, buf_new = pool_mixer(u_pool, buf, start, w_pool, pool_scale)
    mix = jnp.concatenate([hm, zp], axis=-1).astype(x.dtype) @ w_out
    x = x + mix
    x = x + peer_ffn(rmsnorm(x, norm2), peer_wq, peer_keys, peer_u, peer_v)
    x = x + jax.nn.sigmoid(x @ w_gate) * (p.astype(x.dtype) @ w_ple)
    return x, C_new, n_new, m_new, buf_new

def run_trunk(x, p, C0, n0, m0, buf0, start, params, norm_f):
    Cs, ns, ms, bufs = [], [], [], []
    for l in range(DEPTH):
        lw = tuple(w[l] for w in params)
        x, C, n, m, buf = layer(x, p[l], C0[l], n0[l], m0[l], buf0[l], start, *lw)
        Cs.append(C); ns.append(n); ms.append(m); bufs.append(buf)
    y = rmsnorm(x, norm_f)
    return y, jnp.stack(Cs), jnp.stack(ns), jnp.stack(ms), jnp.stack(bufs)

def setup_inputs(seed: int = 0) -> dict:
    key = jax.random.key(seed)
    ks = jax.random.split(key, 24)
    f32 = jnp.float32
    nrm = lambda k, s, sc: jax.random.normal(k, s, f32) * sc
    b_gate = jnp.concatenate([nrm(ks[10], (DEPTH, MLSTM_HEADS), 0.1),
                              3.0 + nrm(ks[11], (DEPTH, MLSTM_HEADS), 0.1)], axis=-1)
    return {
        "x_prompt": nrm(ks[0], (BATCH, SEQ, D_MODEL), 1.0),
        "x_sample": nrm(ks[1], (DEC_BATCH, DEC_SEQ, D_MODEL), 1.0),
        "p_prompt": nrm(ks[2], (DEPTH, BATCH, SEQ, PLE_DIM), 1.0),
        "p_sample": nrm(ks[3], (DEPTH, DEC_BATCH, DEC_SEQ, PLE_DIM), 1.0),
        "state_C": nrm(ks[4], (DEPTH, DEC_BATCH, MLSTM_HEADS, HEAD_DIM, HEAD_DIM), 1.0),
        "state_n": nrm(ks[5], (DEPTH, DEC_BATCH, MLSTM_HEADS, HEAD_DIM), 1.0),
        "state_m": nrm(ks[6], (DEPTH, DEC_BATCH, MLSTM_HEADS), 0.5),
        "state_pool": nrm(ks[7], (DEPTH, DEC_BATCH, POOL_BUF, POOL_WIDTH), 1.0),
        "w_in": nrm(ks[8], (DEPTH, D_MODEL, PROJ_WIDTH), D_MODEL ** -0.5),
        "b_gate": b_gate,
        "mlstm_norm": 1.0 + nrm(ks[9], (DEPTH, MLSTM_WIDTH), 0.05),
        "w_pool": nrm(ks[12], (DEPTH, POOL_GROUPS, POOL_GROUP, POOL_GROUP), POOL_GROUP ** -0.5),
        "pool_scale": 1.0 + nrm(ks[13], (DEPTH, POOL_WIDTH), 0.05),
        "w_out": nrm(ks[14], (DEPTH, MIX_WIDTH, D_MODEL), MIX_WIDTH ** -0.5),
        "norm1": 1.0 + nrm(ks[15], (DEPTH, D_MODEL), 0.05),
        "norm2": 1.0 + nrm(ks[16], (DEPTH, D_MODEL), 0.05),
        "peer_wq": nrm(ks[17], (DEPTH, D_MODEL, PEER_HEADS * PEER_QDIM), D_MODEL ** -0.5),
        "peer_keys": nrm(ks[18], (DEPTH, 2, PEER_HEADS, PEER_NKEYS, PEER_HALF), PEER_HALF ** -0.5),
        "peer_u": nrm(ks[19], (DEPTH, PEER_EXPERTS, D_MODEL), D_MODEL ** -0.5),
        "peer_v": nrm(ks[20], (DEPTH, PEER_EXPERTS, D_MODEL), 0.1),
        "w_ple": nrm(ks[21], (DEPTH, PLE_DIM, D_MODEL), PLE_DIM ** -0.5),
        "w_gate": nrm(ks[22], (DEPTH, D_MODEL, D_MODEL), D_MODEL ** -0.5),
        "norm_f": 1.0 + nrm(ks[23], (D_MODEL,), 0.05),
    }

def reference(x_prompt, x_sample, p_prompt, p_sample, state_C, state_n, state_m, state_pool,
              w_in, b_gate, mlstm_norm, w_pool, pool_scale, w_out, norm1, norm2,
              peer_wq, peer_keys, peer_u, peer_v, w_ple, w_gate, norm_f):
    params = (w_in, b_gate, mlstm_norm, w_pool, pool_scale, w_out, norm1, norm2,
              peer_wq, peer_keys, peer_u, peer_v, w_ple, w_gate)
    f32 = jnp.float32
    C0 = jnp.zeros((DEPTH, BATCH, MLSTM_HEADS, HEAD_DIM, HEAD_DIM), f32)
    n0 = jnp.zeros((DEPTH, BATCH, MLSTM_HEADS, HEAD_DIM), f32)
    m0 = jnp.zeros((DEPTH, BATCH, MLSTM_HEADS), f32)
    buf0 = jnp.zeros((DEPTH, BATCH, POOL_BUF, POOL_WIDTH), f32)
    y_prompt, C_p, n_p, m_p, pool_p = run_trunk(x_prompt, p_prompt, C0, n0, m0, buf0, 0, params, norm_f)
    y_sample, C_s, n_s, m_s, pool_s = run_trunk(x_sample, p_sample, state_C, state_n, state_m, state_pool,
                                                PAST_LEN, params, norm_f)
    return (y_prompt, y_sample, C_p, n_p, m_p, pool_p, C_s, n_s, m_s, pool_s)


_drawn_inputs = setup_inputs


def setup_inputs(seed=0):
    import zlib

    import numpy as np

    out = dict(_drawn_inputs(seed))
    spreads = {}
    factors = {'mlstm_norm': 2.727, 'norm2': 4.615}
    for name, (base, spread) in spreads.items():
        noise = np.random.default_rng([zlib.crc32(name.encode()), seed]).standard_normal(out[name].shape)
        drawn = base * np.exp(spread * noise) if base else spread * noise
        out[name] = __import__('jax').numpy.asarray(drawn.astype(out[name].dtype))
    for name, factor in factors.items():
        out[name] = (out[name] * factor).astype(out[name].dtype)
    return out
```

```python
from contextlib import ExitStack

import concourse.bass as bass
import numpy as np
from concourse import mybir

F32 = mybir.dt.float32
U32 = mybir.dt.uint32
ALU = mybir.AluOpType
ACT = mybir.ActivationFunctionType
AX = mybir.AxisListType.X

DEPTH, SEQ, DEC, D = 2, 256, 8, 1024
HEADS, HD, POOLW = 4, 128, 512
WINDOWS = (2, 4, 8, 16)
TAIL = max(WINDOWS) - 1
PH, NKEYS, EXPERTS, TOPK = 8, 128, 16384, 16
PLE = 256
EPS = 1e-6
P = 128
KT = D // P
BLOCK = 512
IN0, OUT0, PQ0, GATE0, PLE0, HALVES = 0, 10, 14, 22, 26, 27
PAIRS = PH * TOPK
STAIR = [TOPK // (a + 1) for a in range(TOPK)]
CANDS = sum(STAIR)
NEG = -1e30
REMOVED = -3e38

RING = 8
GROUP = 2
DIAGS = 2
WRING = 3
BANKS = 6

_widths = [("ident", P), ("tri", P), ("mask", P), ("ones", P), ("band_a", 4 * P), ("band_b", 4 * P),
           ("band_prev", 4 * P), ("band_buf", 32), ("band_new", 32), ("own", 64), ("own_head", 32), ("key0", 64),
           ("key1", 64), ("copy8", 64), ("own_token", 8), ("place", CANDS), ("eps", 1)]
AT, _at = {}, 0
for _name, _w in _widths:
    AT[_name] = (_at, _w)
    _at += _w
NCONST = _at

KIND = ["A", "B", "S", "A", "B", "S"]
PASS_TILES = [[0], [1, 2], [3], [4, 5]]
ROWS = {"A": P, "B": P, "S": DEC}
LANES = {"A": P, "B": P, "S": PH * DEC}
SLOTS = {"A": PAIRS, "B": PAIRS, "S": TOPK}


def layer_of(tile):
    return tile // 3


def stage_front(p):
    tiles = PASS_TILES[p]
    big, small = tiles[0], tiles[1:]
    out = []

    def add(cost, stage, *key):
        out.append((cost, (stage, *key)))

    if p % 2 == 0:
        add(0, "layer", layer_of(big))
    for t in tiles:
        add(3, "turn", t)
    for t in tiles:
        add(2, "gates", t)
    extra = {1: ["cum"], 2: ["spread"], 3: ["weigh"]}
    for j in range(5):
        for h in range(2):
            add(5, "project", p, j, h)
        for s in extra.get(j, []):
            add(2, s, big)
    add(3, "turn_qk", big)
    add(3, "scores", big)
    add(3, "values", big)
    add(4, "state", big)
    add(4, "heads", big)
    for t in small:
        add(3, "sample_read", t)
        for b in range(DEC):
            add(2, "sample_write", t, b)
        add(3, "heads", t)
    for t in tiles:
        add(3, "pool", t)
    for j in range(2):
        for h in range(2):
            add(5, "mix", p, j, h)
    for t in tiles:
        add(4, "turn2", t)
    for j in range(4):
        for h in range(2):
            add(5, "query", p, j, h)
        for t in tiles:
            add(2, "match", t, j)
        for i in range(4):
            add(2, "rank", big, 4 * j + i)
    for t in tiles:
        if t in small:
            add(2, "rank", t, 0)
        add(3, "pairs", t)
        for h in range(PH if KIND[t] != "S" else 1):
            add(3, "best", t, h)
        add(2, "choose", t)
    return out


def stage_back(p):
    tiles = PASS_TILES[p]
    out = []
    for t in tiles:
        out.append((3, ("turn3", t)))
    for h in range(4):
        out.append((5, ("gate", p, h // 2, h % 2)))
    out.append((4, ("embed", p)))
    if layer_of(tiles[0]) == DEPTH - 1:
        for t in tiles:
            out.append((3, ("final", t)))
    return out


def groups_of(p):
    return [("slots", t, g) for t in PASS_TILES[p] for g in range(SLOTS[KIND[t]] // GROUP)]


def woven(groups, stages):
    total, done, at, out = sum(c for c, _ in stages) or 1, 0, 0, []
    span = len(groups) - 3
    for i, g in enumerate(groups):
        out.append(g)
        while i and at < len(stages) and done < total * (i + 1) / span:
            done += stages[at][0]
            out.append(stages[at][1])
            at += 1
    return out + [s for _, s in stages[at:]]


def make_schedule():
    out = [s for _, s in stage_front(0)]
    out += woven(groups_of(0), stage_front(1))
    out += woven(groups_of(1), stage_back(0) + stage_front(2))
    out += woven(groups_of(2), stage_back(1) + stage_front(3))
    out += woven(groups_of(3), stage_back(2))
    out += [("flush",)] + [s for _, s in stage_back(3)]
    return out


SCHEDULE = make_schedule()


def count(stages, entry):
    n = 0
    for e in SCHEDULE:
        n += e[0] in stages
        if e == entry:
            return n
    raise KeyError(entry)


RMS_STAGES = ("turn", "turn2", "final")

FIRST_SLOT = {}
_n = 0
for _p in range(4):
    for _t in PASS_TILES[_p]:
        FIRST_SLOT[_t] = _n
        _n += SLOTS[KIND[_t]]
ALL_SLOTS = _n

HALF_OF = {}
for _e in SCHEDULE:
    if _e[0] in ("project", "mix", "query", "gate", "embed"):
        HALF_OF[_e] = len(HALF_OF)
HALVES_IN_ORDER = list(HALF_OF)


def half_index(e):
    if e[0] == "embed":
        return PLE0
    return {"project": IN0, "mix": OUT0, "query": PQ0, "gate": GATE0}[e[0]] + 2 * e[2] + e[3]


def build(nc, a):
    with ExitStack() as ctx:
        def sb(name, *shape, dt=F32):
            return ctx.enter_context(nc.sbuf_tensor(name, list(shape), dt))

        def sem(name):
            return ctx.enter_context(nc.semaphore(name))

        consts = sb("consts", P, NCONST)

        def const(name, rows=P):
            lo, w = AT[name]
            return consts[0:rows, lo:lo + w]

        x = {"A": sb("x_a", P, D), "B": sb("x_b", P, D), "S": sb("x_s", DEC, D)}
        xn = {"A": sb("xn_a", P, D), "B": sb("xn_b", P, D), "S": sb("xn_s", PH * DEC, D)}
        turned = {"A": sb("turned", P, KT, P), "S": sb("turned_s", P, KT, DEC)}
        wring = sb("wring", P, WRING, 4, BLOCK)
        rows = sb("rows", P, RING, 2 * D)
        gain2 = sb("gain2", P, D)
        keys = sb("keys", P, 2 * PH, NKEYS)
        w_gates = sb("w_gates", P, DEPTH, KT, 8)
        b_gates = sb("b_gates", P, DEPTH, 8)
        w_pool = sb("w_pool", P, 4, P)
        cols = sb("cols", P, DEPTH, 24)
        emb = sb("emb", P, 2, P + DEC)
        qk = sb("qk", P, 2, 512)
        q = {"A": qk[:, 0, :], "S": sb("q_s", DEC, 512)}
        k = {"A": qk[:, 1, :], "S": sb("k_s", DEC, 512)}
        v = {"A": sb("v", P, HEADS, HD + 1), "S": sb("v_s", DEC, HEADS, HD + 1)}
        o = {"A": sb("o", P, 512), "S": sb("o_s", DEC, 512)}
        u_in = {"A": sb("u_a", P, 512), "B": sb("u_b", P, 512), "S": sb("u_s", DEC, 512)}
        inv1 = {"A": sb("inv1", P, 2), "S": sb("inv1_s", DEC, 2)}
        inv2 = {"A": sb("inv2", P, 2), "S": sb("inv2_s", DEC, 2)}
        g8 = {"A": sb("g8", P, 8), "S": sb("g8_s", DEC, 8)}
        lf = {"A": sb("lf", P, 4), "S": sb("lf_s", DEC, 4)}
        for of_kind in (turned, q, k, v, o, inv1, inv2, g8, lf):
            of_kind["B"] = of_kind["A"]
        qT, kT = sb("q_t", P, HEADS, P), sb("k_t", P, HEADS, P)
        decayed = sb("decayed", P, HEADS, P)
        state = sb("state", P, HEADS, HD + 1)
        mixer = sb("mixer", P, 2 * HEADS * HD + 2 * HEADS * (HD + 1))
        prod, junk = (mixer[:, i * 512:(i + 1) * 512].rearrange("p (h c) -> p h c", h=HEADS) for i in range(2))
        inter, num = (mixer[:, 1024 + i * 516:1024 + (i + 1) * 516].rearrange("p (h c) -> p h c", h=HEADS)
                      for i in range(2))
        scratch = sb("scratch", P, DEC * HEADS * (HD + 1))
        cs = scratch[:, :].rearrange("p (s e) -> p s e", e=HD + 1)
        match = scratch[:, 0:2048]
        onehot = scratch[:, 2048:2848].rearrange("p (k c) -> p k c", c=CANDS)
        match_s = scratch[:, 3648:3648 + NKEYS]
        pool_buf = sb("pool_buf", DEC * TAIL, POOLW)
        ga, gb, gc = sb("gate_abs_f", P, 4), sb("gate_exp_f", P, 4), sb("gate_ln_f", P, 4)
        lead = sb("lead", P, 4)
        mb = sb("mb", P, 8)
        neg_m = sb("neg_m", P, 4)
        m_prev = sb("m_prev", P, 4)
        last = sb("last_mb", P, 8)
        args1, exps1 = sb("args1", P, 12), sb("exps1", P, 12)
        args2, exps2 = sb("args2", P, 8), sb("exps2", P, 8)
        w_own = sb("w_own", DEC, DEC, 4)
        w_spread = sb("w_spread", P, 32)
        qk_s = sb("qk_s", DEC, 4)
        m_s = sb("m_s", DEC, DEPTH, 4)
        m_s_new = sb("m_s_new", DEC, 4)
        q_own = sb("q_own", P, HEADS, DEC, DEC)
        den = sb("den", P, 4)
        h_in, h_root, h_inv = sb("h_in", P, 4), sb("h_root", P, 4), sb("h_inv", P, 4)
        r_in, r_root = sb("r_in", P, 1), sb("r_root", P, 1)
        inv_rep = sb("inv_rep", PH * DEC, 1)
        pq, pqT = qk, qT
        pqT_s = mixer[:, 0:2048].rearrange("p (n t) -> p n t", t=P)
        top, top_f = (kT[:, 2 * i:2 * i + 2, :].rearrange("p h (n k) -> p (h n) k", k=TOPK) for i in range(2))
        top_i = sb("top_i", P, 2 * PH, TOPK, dt=U32)
        pair_s = sb("pair_s", PH * DEC, 4, TOPK)
        base, best, best_f, chosen = (decayed[:, i, :].rearrange("p (h k) -> p h k", k=TOPK) for i in range(4))
        sums, codes = (scratch[:, 2848 + i * 400:2848 + (i + 1) * 400].rearrange("p (h c) -> p h c", c=CANDS)
                       for i in range(2))
        best_i = sb("best_i", P, PH, TOPK, dt=U32)
        shares = sb("shares", P, PH)
        index = {t: sb(f"index_{t}", LANES[t], SLOTS[t], dt=U32) for t in "ABS"}
        prob = {t: sb(f"prob_{t}", LANES[t], SLOTS[t]) for t in "ABS"}
        dots = {t: sb(f"dots_{t}", LANES[t], SLOTS[t]) for t in "ABS"}
        gel = sb("gel", P, 4, GROUP)
        wts = sb("wts", P, 4, GROUP)
        diag = sb("diag", P, DIAGS, GROUP, P)

        acc = ctx.enter_context(nc.psum_tensor("acc", [P, 2, BLOCK], F32))
        banks = [ctx.enter_context(nc.psum_tensor(f"bank{i}", [P, BLOCK], F32)) for i in range(BANKS)]

        consts_in, small_in, x_in = sem("consts_in"), sem("small_in"), sem("x_in")
        layer_in, emb_in, states_in = sem("layer_in"), sem("emb_in"), sem("states_in")
        half_in = [sem(f"half_in{i}") for i in range(WRING)]
        row_in = [sem(f"row_in{i}") for i in range(RING)]
        prompt_stored, samples_stored, stored = sem("prompt_stored"), sem("samples_stored"), sem("stored")
        bank_full = [sem(f"bank_full{i}") for i in range(BANKS)]
        bank_free = [sem(f"bank_free{i}") for i in range(BANKS)]
        half_used, slot_used = sem("half_used"), sem("slot_used")
        vector_step, scalar_step = sem("vector_step"), sem("scalar_step")
        ones_set, zeros_set = sem("ones_set"), sem("zeros_set")
        inv_ready, gate_abs, lf_ready = sem("inv_ready"), sem("gate_abs"), sem("lf_ready")
        lead_diag, decay_args, args1_ready = sem("lead_diag"), sem("decay_args"), sem("args1_ready")
        args2_ready, k_weighted, state_written = sem("args2_ready"), sem("k_weighted"), sem("state_written")
        head_var, heads_ready = sem("head_var"), sem("heads_ready")
        sample_args, w_own_ready = sem("sample_args"), sem("w_own_ready")
        sample_k, sample_state = sem("sample_k"), sem("sample_state")
        pair_src, logits_ready, index_ready = sem("pair_src"), sem("logits_ready"), sem("index_ready")
        dot_done, weight_done, acc_read = sem("dot_done"), sem("weight_done"), sem("acc_read")
        x_gated, x_final = sem("x_gated"), sem("x_final")
        root_ready, gate_ln, decay_done = sem("root_ready"), sem("gate_ln"), sem("decay_done")
        exps1_ready, exps2_ready, sample_exp = sem("exps1_ready"), sem("exps2_ready"), sem("sample_exp")
        head_root, logits_exp = sem("head_root"), sem("logits_exp")
        gelu_done, diag_done = sem("gelu_done"), sem("diag_done")

        use, uses = {}, []

        def rows_of(t):
            return ROWS[KIND[t]]

        def heads_view(ap, m, n=HEADS):
            return ap.rearrange("p (h c) -> p h c", h=n)

        def across(ap, n):
            m, h = ap.shape
            return ap.rearrange("p (h o) -> p h o", o=1).to_broadcast([m, h, n])

        def down(ap, n):
            m, c = ap.shape
            return ap.rearrange("p (o c) -> p o c", o=1).to_broadcast([m, n, c])

        block = ctx.enter_context(nc.Block())

        def emptied(eng, *name):
            b, n = use[name]
            eng.wait_ge(bank_free[b], n + 1)

        @block.tensor
        def _(pe):
            def opened(*name):
                b, n = len(uses) % BANKS, len(uses) // BANKS
                uses.append(name)
                use[name] = (b, n)
                if n:
                    pe.wait_ge(bank_free[b], n)
                return banks[b]

            def closed(ins, *name):
                ins.then_inc(bank_full[use[name][0]], 1)

            def half(e):
                n = HALF_OF[e]
                pe.wait_ge(half_in[n % WRING], 16 * (n // WRING + 1))
                return wring[:, n % WRING]

            def turn_rows(name, t):
                m, src = rows_of(t), x[KIND[t]]
                n = 1 if KIND[t] == "S" else 2
                for i in range(n):
                    ps = opened(name, t, i)
                    for c in range(KT // n):
                        lo = (i * KT // n + c) * P
                        ins = pe.transpose(ps[:, c * m:(c + 1) * m], src[:, lo:lo + P], const("ident", m)[:, 0:m])
                    closed(ins, name, t, i)

            def dense(name, p, j, h, source, parts):
                w = half((name, p, j, h))
                for t in PASS_TILES[p]:
                    m = rows_of(t)
                    if h == 0:
                        if j == 0:
                            for s in source:
                                for i in range(1 if KIND[t] == "S" or not parts else 2):
                                    emptied(pe, *((s, t, i) if parts else (s, t)))
                        ps = opened(name, t, j)
                    else:
                        ps = banks[use[(name, t, j)][0]]
                    for c in range(4):
                        ins = pe.matmul(ps[0:m, :], turned[KIND[t]][:, 4 * h + c, 0:m], w[:, c, :],
                                        start=(h == 0 and c == 0), stop=(h == 1 and c == 3), skip_group_check=True)
                    if h == 1:
                        closed(ins, name, t, j)
                if h == 0:
                    ins.then_inc(half_used, 1)

            def turn(t):
                if t == 0:
                    pe.wait_ge(x_in, 48)
                    pe.wait_ge(consts_in, 16)
                if t >= 3:
                    pe.wait_ge(x_gated, t - 2)
                turn_rows("turn", t)

            def gates(t):
                m = rows_of(t)
                if t == 0:
                    pe.wait_ge(small_in, 16 * 4)
                for i in range(1 if KIND[t] == "S" else 2):
                    emptied(pe, "turn", t, i)
                ps = opened("gates", t)
                for c in range(KT):
                    ins = pe.matmul(ps[0:m, 0:8], turned[KIND[t]][:, c, 0:m], w_gates[:, layer_of(t), c, :],
                                    start=(c == 0), stop=(c == KT - 1))
                closed(ins, "gates", t)

            def project(p, j, h):
                dense("project", p, j, h, ("turn",), True)

            def cumulate(t):
                pe.wait_ge(lf_ready, t + 1)
                ps = opened("cum", t)
                closed(pe.matmul(ps[:, 0:4], const("tri"), lf["A"][:, :], start=True, stop=True), "cum", t)

            def spread(t):
                pe.wait_ge(lead_diag, count(("cum",), ("cum", t)))
                ps = opened("spread", t)
                closed(pe.matmul(ps[:, :], const("ones"), prod[:, :, :].rearrange("p h s -> p (h s)"),
                                 start=True, stop=True), "spread", t)

            def turn_qk(t):
                for j, name, src in ((0, "turn_q", q["A"]), (1, "turn_k", k["A"])):
                    emptied(pe, "project", t, j)
                    ps = opened(name, t)
                    for h in range(HEADS):
                        ins = pe.transpose(ps[:, h * P:(h + 1) * P], src[:, h * P:(h + 1) * P], const("ident"))
                    closed(ins, name, t)

            def scores(t):
                emptied(pe, "turn_q", t)
                emptied(pe, "turn_k", t)
                ps = opened("scores", t)
                for h in range(HEADS):
                    ins = pe.matmul(ps[:, h * P:(h + 1) * P], qT[:, h, :], kT[:, h, :], start=True, stop=True)
                closed(ins, "scores", t)

            def by_pairs(name, t, lhs, rhs):
                for i in range(2):
                    ps = opened(name, t, i)
                    for h in range(2):
                        ins = pe.matmul(ps[:, h * 129:h * 129 + 129], lhs[:, 2 * i + h, :], rhs[:, 2 * i + h, :],
                                        start=True, stop=True)
                    closed(ins, name, t, i)

            def values(t):
                emptied(pe, "scores", t)
                ps = opened("turn_prod", t)
                for h in range(HEADS):
                    ins = pe.transpose(ps[:, h * P:(h + 1) * P], prod[:, h, :], const("ident"))
                closed(ins, "turn_prod", t)
                if KIND[t] == "B":
                    emptied(pe, "state", t - 1, 1)
                    by_pairs("inter", t, qT, state)
                emptied(pe, "turn_prod", t)
                emptied(pe, "project", t, 2)
                by_pairs("values", t, decayed, v["A"])

            def state_update(t):
                pe.wait_ge(decay_args, count(("spread",), ("spread", t)))
                ps = opened("last", t)
                closed(pe.matmul(ps[:, 0:8], const("ident")[:, P - 1:P].to_broadcast([P, P]), mb[:, :], start=True, stop=True), "last", t)
                pe.wait_ge(k_weighted, count(("state",), ("state", t)))
                by_pairs("state", t, prod, v["A"])

            def sample_read(t):
                n = layer_of(t) + 1
                emptied(pe, "project", t, 0)
                ps = opened("turn_qs", t)
                for h in range(HEADS):
                    ins = pe.transpose(ps[:, h * DEC:(h + 1) * DEC], q["S"][:, h * P:(h + 1) * P],
                                       const("ident", DEC)[:, 0:DEC])
                closed(ins, "turn_qs", t)
                pe.wait_ge(w_own_ready, n)
                ps = opened("w_spread", t)
                closed(pe.matmul(ps[:, 0:32], const("ones", DEC), w_own[:, :, :].rearrange("p b h -> p (b h)"),
                                 start=True, stop=True), "w_spread", t)
                emptied(pe, "turn_qs", t)
                pe.wait_ge(states_in, 32 * n)
                for i in range(2):
                    ps = opened("read", t, i)
                    for h in range(2):
                        for b in range(DEC):
                            ins = pe.matmul(ps[0:DEC, h * 129:h * 129 + 129], q_own[:, 2 * i + h, b, :],
                                            cs[:, b * HEADS + 2 * i + h, :], start=(b == 0), stop=(b == DEC - 1))
                    closed(ins, "read", t, i)

            def sample_write(t, b):
                pe.wait_ge(sample_k, count(("sample_write",), ("sample_write", t, b)))
                emptied(pe, "project", t, 2)
                for i in range(2):
                    ps = opened("write", t, b, i)
                    for h in range(2):
                        hh = 2 * i + h
                        ins = pe.matmul(ps[:, h * 129:h * 129 + 129], pq[0:DEC, b % 2, hh * P:(hh + 1) * P],
                                        v["S"][:, hh, :], start=True, stop=True)
                    closed(ins, "write", t, b, i)

            def heads(t):
                m = rows_of(t)
                pe.wait_ge(heads_ready, t + 1)
                ps = opened("heads", t)
                for h in range(HEADS):
                    ins = pe.transpose(ps[:, h * m:(h + 1) * m], num[0:m, h, 0:HD], const("ident", m)[:, 0:m])
                closed(ins, "heads", t)

            def pool(t):
                m, kind = rows_of(t), KIND[t]
                emptied(pe, "project", t, 4)
                ps = opened("pool_r", t)
                for g in range(4):
                    out, col = ps[:, g * m:(g + 1) * m], slice(g * P, (g + 1) * P)
                    if kind == "A":
                        ins = pe.matmul(out, u_in["A"][:, col], const("band_a")[:, col], start=True, stop=True)
                    elif kind == "B":
                        pe.matmul(out, u_in["A"][:, col], const("band_prev")[:, col], start=True, stop=False)
                        ins = pe.matmul(out, u_in["B"][:, col], const("band_b")[:, col], start=False, stop=True)
                    else:
                        pe.wait_ge(states_in, 32 * (layer_of(t) + 1))
                        pe.matmul(out, pool_buf[:, col], const("band_buf", DEC * TAIL)[:, g * 8:g * 8 + 8],
                                  start=True, stop=False)
                        ins = pe.matmul(out, u_in["S"][:, col], const("band_new", DEC)[:, g * 8:g * 8 + 8],
                                        start=False, stop=True)
                closed(ins, "pool_r", t)
                emptied(pe, "pool_r", t)
                pe.wait_ge(layer_in, 48 * (layer_of(t) + 1))
                ps = opened("pool_z", t)
                for g in range(4):
                    ins = pe.matmul(ps[:, g * m:(g + 1) * m], w_pool[:, g, :], decayed[:, g, 0:m],
                                    start=True, stop=True)
                closed(ins, "pool_z", t)

            def mix(p, j, h):
                dense("mix", p, j, h, ("heads", "pool_z"), False)

            def turn2(t):
                emptied(pe, "mix", t, 0)
                emptied(pe, "mix", t, 1)
                turn_rows("turn2", t)
                if KIND[t] == "S":
                    for i in range(2):
                        ps = opened("rep", t, i)
                        closed(pe.matmul(ps[0:64, :], const("copy8", DEC), x["S"][:, i * BLOCK:(i + 1) * BLOCK],
                                         start=True, stop=True), "rep", t, i)
                    pe.wait_ge(inv_ready, count(RMS_STAGES, ("turn2", t)))
                    ps = opened("rep_inv", t)
                    closed(pe.matmul(ps[0:64, 0:2], const("copy8", DEC), inv2["S"][:, :], start=True, stop=True),
                           "rep_inv", t)

            def query(p, j, h):
                dense("query", p, j, h, ("turn2",), True)

            def match_keys(t, j):
                m, kind = rows_of(t), KIND[t]
                emptied(pe, "query", t, j)
                ps = opened("turn_pq", t, j)
                for i in range(4):
                    ins = pe.transpose(ps[:, i * m:(i + 1) * m], pq[0:m, 1 if kind == "S" else 0, i * P:(i + 1) * P],
                                       const("ident", m)[:, 0:m])
                closed(ins, "turn_pq", t, j)
                emptied(pe, "turn_pq", t, j)
                if j == 0:
                    pe.wait_ge(layer_in, 48 * (layer_of(t) + 1))
                if kind != "S":
                    ps = opened("match", t, j)
                    for i in range(4):
                        ins = pe.matmul(ps[:, i * P:(i + 1) * P], pqT[:, i, :], keys[:, 4 * j + i, :], start=True, stop=True)
                    closed(ins, "match", t, j)
                elif j == 3:
                    ps = opened("match", t, j)
                    for i in range(2 * PH):
                        ins = pe.matmul(ps[:, 0:P], pqT_s[:, i, :], keys[:, i, :], start=(i == 0), stop=(i == 2 * PH - 1))
                    closed(ins, "match", t, j)

            def pairs(t):
                if KIND[t] != "S":
                    return
                pe.wait_ge(pair_src, layer_of(t) + 1)
                ps = opened("pairs", t)
                for c in range(2):
                    pe.matmul(ps[0:64, c * 32:c * 32 + 16], const(f"key{c}"), top[:, 0, :], start=True, stop=True)
                    ins = pe.matmul(ps[0:64, c * 32 + 16:c * 32 + 32], const(f"key{c}"), top_f[:, 0, :],
                                    start=True, stop=True)
                closed(ins, "pairs", t)

            def add_values(t, g):
                kind = KIND[t]
                m, lanes, n = ROWS[kind], LANES[kind], FIRST_SLOT[t] // GROUP + g
                if g == 0 and t > 0:
                    pe.wait_ge(acc_read, t)
                pe.wait_ge(diag_done, n + 1)
                for i in range(GROUP):
                    s = g * GROUP + i
                    for c in range(2):
                        lo = D + c * BLOCK
                        ins = pe.matmul(acc[0:m, c, :], diag[0:lanes, n % DIAGS, i, 0:m],
                                        rows[0:lanes, (n * GROUP + i) % RING, lo:lo + BLOCK],
                                        start=(s == 0), stop=(s == SLOTS[kind] - 1), skip_group_check=True)
                    ins.then_inc(slot_used, 1)

            def turn3(t):
                pe.wait_ge(acc_read, t + 1)
                turn_rows("turn3", t)

            def gate(p, j, h):
                dense("gate", p, j, h, ("turn3",), True)

            def embed(p):
                w = half(("embed", p))
                pe.wait_ge(emb_in, 16 * (p + 1))
                for t in PASS_TILES[p]:
                    m = rows_of(t)
                    lo = P if KIND[t] == "S" else 0
                    for j in range(2):
                        ps = opened("embed", t, j)
                        for c in range(2):
                            ins = pe.matmul(ps[0:m, :], emb[:, c, lo:lo + m], w[:, 2 * j + c, :],
                                            start=(c == 0), stop=(c == 1))
                        closed(ins, "embed", t, j)

            do = {"turn": turn, "gates": gates, "project": project, "cum": cumulate, "spread": spread,
                  "turn_qk": turn_qk, "scores": scores, "values": values, "state": state_update,
                  "sample_read": sample_read, "sample_write": sample_write, "heads": heads, "pool": pool, "mix": mix,
                  "turn2": turn2, "query": query, "match": match_keys, "pairs": pairs, "turn3": turn3, "gate": gate,
                  "embed": embed}
            late = None
            for e in SCHEDULE:
                if e[0] in ("slots", "flush"):
                    if late:
                        add_values(*late)
                    late = e[1:]
                elif e[0] in do:
                    do[e[0]](*e[1:])

        def reader(eng, step_sem):
            counts = {}

            def after(ins, s=step_sem):
                counts[s.name] = counts.get(s.name, 0) + 1
                ins.then_inc(s, 1)
                eng.wait_ge(s, counts[s.name])

            def full(*name):
                b, n = use[name]
                eng.wait_ge(bank_full[b], n + 1)
                return banks[b]

            def free(ins, *name):
                b, n = use[name]
                ins.then_inc(bank_free[b], 1)
                eng.wait_ge(bank_free[b], n + 1)

            return after, full, free

        @block.sync
        def _(sp):
            sp.dma_start(consts[:, :], a["consts"]).then_inc(consts_in, 16)
            for kind, lo, m in (("A", 0, P), ("B", P, P), ("S", SEQ, DEC)):
                sp.dma_start(x[kind][:, :], a["x"][lo:lo + m, :]).then_inc(x_in, 16)
            sp.dma_start(w_gates[:, :, :, :].rearrange("p l c n -> p (l c n)"), a["w_gates"]).then_inc(small_in, 16)
            sp.dma_start(b_gates[:, :, :].rearrange("p l n -> p (l n)"), a["b_gates"]).then_inc(small_in, 16)
            sp.dma_start(cols[:, :, :].rearrange("p l n -> p (l n)"), a["cols"]).then_inc(small_in, 16)
            sp.dma_start(m_s[:, :, :].rearrange("p l h -> p (l h)"), a["m_s"]).then_inc(small_in, 16)

            def load_half(e):
                n = HALF_OF[e]
                if n >= WRING:
                    old = HALVES_IN_ORDER[n - WRING]
                    last_tile = PASS_TILES[old[1]][-1]
                    if old[0] == "embed" or old[3] == 1:
                        name = ("embed", last_tile, 1) if old[0] == "embed" else (old[0], last_tile, old[2])
                        sp.wait_ge(bank_full[use[name][0]], use[name][1] + 1)
                    else:
                        sp.wait_ge(half_used, sum(f[0] != "embed" and f[3] == 0 for f in HALVES_IN_ORDER[:n - WRING + 1]))
                layer = layer_of(PASS_TILES[e[1]][0])
                sp.dma_start(wring[:, n % WRING].rearrange("p c n -> p (c n)"),
                             a["w"][layer, half_index(e)]).then_inc(half_in[n % WRING], 16)

            for e in SCHEDULE:
                if e in HALF_OF:
                    load_half(e)
                if e[0] == "layer":
                    layer = e[1]
                    if layer:
                        sp.wait_ge(index_ready, 3)
                    sp.dma_start(keys[:, :, :].rearrange("p a b -> p (a b)"), a["keys"][layer]).then_inc(layer_in, 16)
                    sp.dma_start(gain2[:, :], a["gain"][layer]).then_inc(layer_in, 16)
                    sp.dma_start(w_pool[:, :, :].rearrange("p g n -> p (g n)"), a["w_pool"][layer]).then_inc(layer_in, 16)
                if e[0] == "turn" and KIND[e[1]] == "S":
                    layer = layer_of(e[1])
                    sp.wait_ge(index_ready, e[1] - 1)
                    sp.dma_start(scratch[:, :], a["c_s"][layer]).then_inc(states_in, 16)
                    sp.dma_start(pool_buf[:, :], a["pool_buf"][layer]).then_inc(states_in, 16)
                    sp.dma_start(a["out_pool_s"][layer, :, 0:TAIL - 1, :], a["pool_old"][layer, :, 1:TAIL, :]).then_inc(stored, 16)
                if e[0] == "state" and KIND[e[1]] == "B":
                    layer = layer_of(e[1])
                    sp.wait_ge(state_written, count(("state",), e))
                    sp.dma_start(a["out_c_p"][layer], state[:, :, :].rearrange("p h e -> p (h e)")).then_inc(prompt_stored, 16)
                    sp.dma_start(a["out_m_p"][layer:layer + 1, :], m_prev[0:1, :]).then_inc(prompt_stored, 16)
                if e[0] == "sample_write" and e[2] == DEC - 1:
                    layer = layer_of(e[1])
                    sp.wait_ge(sample_state, layer + 1)
                    sp.dma_start(a["out_c_s"][layer], scratch[:, :]).then_inc(samples_stored, 16)
                    sp.dma_start(a["out_m_s"][layer], m_s_new[:, :]).then_inc(samples_stored, 16)
                if e[0] == "pool" and KIND[e[1]] in "BS":
                    layer, kind = layer_of(e[1]), KIND[e[1]]
                    emptied(sp, "project", e[1], 4)
                    if kind == "B":
                        sp.dma_start(a["out_pool_p"][layer], u_in["B"][P - TAIL:P, :]).then_inc(prompt_stored, 16)
                    else:
                        sp.dma_start(a["out_pool_s"][layer, :, TAIL - 1, :], u_in["S"][:, :]).then_inc(samples_stored, 16)
                if e[0] == "gate" and e[2:] == (0, 0):
                    p, layer = e[1], layer_of(PASS_TILES[e[1]][0])
                    lo, n = ((0, P), (P, P + DEC))[p % 2]
                    if p:
                        b, i = use[("embed", PASS_TILES[p - 1][-1], 1)]
                        sp.wait_ge(bank_full[b], i + 1)
                    sp.dma_start(emb[:, :, 0:n], a["emb"][layer, :, :, lo:lo + n]).then_inc(emb_in, 16)
                if e == ("turn3", 3):
                    sp.wait_ge(index_ready, 6)
                    sp.dma_start(gain2[:, :], a["gain"][DEPTH]).then_inc(layer_in, 16)
                if e[0] == "final":
                    kind = KIND[e[1]]
                    sp.wait_ge(x_final, count(("final",), e))
                    lo = {"A": 0, "B": P, "S": SEQ}[kind]
                    sp.dma_start(a["out_y"][lo:lo + ROWS[kind], :], x[kind][:, :]).then_inc(stored, 16)
            sp.wait_ge(stored, 16 * (DEPTH + 3))
            sp.wait_ge(prompt_stored, 48 * DEPTH)
            sp.wait_ge(samples_stored, 48 * DEPTH)

        @block.gpsimd
        def _(pool):
            for t in range(6):
                kind = KIND[t]
                pool.wait_ge(index_ready, t + 1)
                for s in range(SLOTS[kind]):
                    n = FIRST_SLOT[t] + s
                    if n >= RING:
                        pool.wait_ge(slot_used, n - RING + 1)
                    pool.indirect_dma_start(
                        out=rows[0:LANES[kind], n % RING, :], out_offset=None, in_=a["uv"],
                        in_offset=bass.IndirectOffsetOnAxis(ap=index[kind][:, s:s + 1], axis=0),
                    ).then_inc(row_in[n % RING], 16)

        @block.scalar
        def _(act):
            after, full, free = reader(act, scalar_step)

            def rms(e, t):
                m, kind, n = rows_of(t), KIND[t], count(RMS_STAGES, e)
                after(act.activation(xn[kind][0:m, :], x[kind][0:m, :], ACT.Square, accum_out=r_in[0:m, :]))
                if n > 1:
                    act.wait_ge(inv_ready, n - 1)
                after(act.activation(r_root[0:m, :], r_in[0:m, :], ACT.Sqrt, scale=1.0 / D, bias=const("eps", m)),
                      root_ready)

            def turn(t):
                if t == 0:
                    act.wait_ge(x_in, 48)
                    act.wait_ge(consts_in, 16)
                if t >= 3:
                    act.wait_ge(x_gated, t - 2)
                rms(("turn", t), t)

            def gates(t):
                m = rows_of(t)
                act.wait_ge(gate_abs, t + 1)
                after(act.activation(gb[0:m, :], ga[0:m, :], ACT.Exp, scale=-1.0))
                after(act.activation(gc[0:m, :], gb[0:m, :], ACT.Ln, bias=1.0), gate_ln)

            def project(p, j, h):
                if h == 0:
                    return
                for t in PASS_TILES[p]:
                    m, kind = rows_of(t), KIND[t]
                    if j == 0:
                        act.wait_ge(inv_ready, count(RMS_STAGES, ("turn", t)))
                    if (t, j) == (0, 2):
                        act.wait_ge(ones_set, 1)
                    if j == 4 and KIND[t] in "BS" and t >= 3:
                        act.wait_ge(prompt_stored if KIND[t] == "B" else samples_stored, 48)
                    ps = full("project", t, j)
                    scale = inv1[kind][:, 1:2] if j == 1 else inv1[kind][:, 0:1]
                    if j == 3:
                        ins = act.activation(o[kind][:, :], ps[0:m, :], ACT.Sigmoid, scale=scale)
                    elif j == 2:
                        ins = act.activation(v[kind][:, :, 0:HD], heads_view(ps[0:m, :], m), ACT.Copy, scale=scale)
                    else:
                        ins = act.activation({0: q, 1: k, 4: u_in}[j][kind][:, :], ps[0:m, :], ACT.Copy, scale=scale)
                    free(ins, "project", t, j)

            def copied(dst, *name):
                free(act.activation(dst, full(*name)[:, :], ACT.Copy), *name)

            def weigh(t):
                act.wait_ge(decay_args, count(("spread",), ("spread", t)))
                for h in range(HEADS):
                    after(act.activation(decayed[:, h, :], decayed[:, h, :], ACT.Exp, bias=neg_m[:, h:h + 1]),
                          *([decay_done] if h == HEADS - 1 else []))
                act.wait_ge(args1_ready, count(("weigh",), ("weigh", t)))
                after(act.activation(exps1[:, 0:8], args1[:, 0:8], ACT.Exp), exps1_ready)

            def turn_qk(t):
                copied(qT[:, :, :].rearrange("p h t -> p (h t)"), "turn_q", t)
                copied(kT[:, :, :].rearrange("p h t -> p (h t)"), "turn_k", t)

            def values(t):
                copied(decayed[:, :, :].rearrange("p h t -> p (h t)"), "turn_prod", t)
                if KIND[t] == "B":
                    for i in range(2):
                        ps = full("inter", t, i)
                        for h in range(2):
                            hh = 2 * i + h
                            ins = act.activation(inter[:, hh, :], ps[:, h * 129:h * 129 + 129], ACT.Copy,
                                                 scale=exps1[:, hh:hh + 1])
                            if h == 0:
                                after(ins)
                        free(ins, "inter", t, i)

            def state_update(t):
                act.wait_ge(args2_ready, count(("state",), ("state", t)))
                after(act.activation(exps2[:, :], args2[:, :], ACT.Exp), exps2_ready)

            def sample_read(t):
                act.wait_ge(sample_args, layer_of(t) + 1)
                after(act.activation(exps1[0:DEC, :], args1[0:DEC, :], ACT.Exp), sample_exp)

            def heads(t):
                m = rows_of(t)
                act.wait_ge(head_var, t + 1)
                after(act.activation(h_root[0:m, :], h_in[0:m, :], ACT.Sqrt, scale=1.0 / HD, bias=const("eps", m)),
                      head_root)

            def pool(t):
                m = rows_of(t)
                ps = full("pool_r", t)
                free(act.activation(decayed[:, :, 0:m], heads_view(ps[:, 0:4 * m], m), ACT.Copy), "pool_r", t)

            def turn2(t):
                emptied(act, "mix", t, 0)
                emptied(act, "mix", t, 1)
                rms(("turn2", t), t)

            def query(p, j, h):
                if h == 0:
                    return
                for t in PASS_TILES[p]:
                    m, kind = rows_of(t), KIND[t]
                    if j == 0:
                        act.wait_ge(inv_ready, count(RMS_STAGES, ("turn2", t)))
                    ps = full("query", t, j)
                    free(act.activation(pq[0:m, 1 if kind == "S" else 0, :], ps[0:m, :], ACT.Copy,
                                        scale=inv2[kind][:, 0:1]), "query", t, j)

            def match_keys(t, j):
                m, kind = rows_of(t), KIND[t]
                ps = full("turn_pq", t, j)
                if kind == "S":
                    act.wait_ge(zeros_set, layer_of(t) + 1)
                    for i in range(4):
                        n = 4 * j + i
                        ins = act.activation(pqT_s[:, n, n * DEC:(n + 1) * DEC], ps[:, i * m:(i + 1) * m], ACT.Copy)
                        if i < 3:
                            after(ins)
                else:
                    ins = act.activation(pqT[:, :, :].rearrange("p h t -> p (h t)"), ps[:, :], ACT.Copy)
                free(ins, "turn_pq", t, j)
                if kind == "B" and j == 0:
                    act.wait_ge(samples_stored, 48 * (layer_of(t) + 1))
                if kind != "S":
                    copied(match[:, j * 512:(j + 1) * 512], "match", t, j)
                elif j == 3:
                    ps = full("match", t, j)
                    free(act.activation(match_s, ps[:, 0:P], ACT.Copy), "match", t, j)

            def choose(t):
                m, hs = LANES[KIND[t]], 1 if KIND[t] == "S" else PH
                act.wait_ge(logits_ready, t + 1)
                after(act.activation(best[0:m, 0:hs, :], best[0:m, 0:hs, :], ACT.Exp), logits_exp)

            def weights(t, g):
                kind = KIND[t]
                m, lanes, n = ROWS[kind], LANES[kind], FIRST_SLOT[t] // GROUP + g
                act.wait_ge(dot_done, n + 1)
                after(act.activation(gel[0:lanes, n % 4, :], dots[kind][:, g * GROUP:(g + 1) * GROUP],
                                     ACT.Gelu_apprx_tanh), gelu_done)
                act.wait_ge(weight_done, n + 1)
                if n >= DIAGS:
                    act.wait_ge(slot_used, (n - DIAGS + 1) * GROUP)
                for i in range(GROUP):
                    own = const("own_token", lanes) if kind == "S" else const("ident")
                    after(act.activation(diag[0:lanes, n % DIAGS, i, 0:m], own, ACT.Copy, scale=wts[0:lanes, n % 4, i:i + 1]),
                          *([diag_done] if i == GROUP - 1 else []))

            def turn3(t):
                m, n = rows_of(t), 1 if KIND[t] == "S" else 2
                for i in range(n):
                    ps = full("turn3", t, i)
                    c = KT // n
                    free(act.activation(turned[KIND[t]][:, i * c:(i + 1) * c, :],
                                        ps[:, 0:c * m].rearrange("p (h c) -> p h c", h=c), ACT.Copy), "turn3", t, i)

            def gate(p, j, h):
                if h == 0:
                    return
                for t in PASS_TILES[p]:
                    m, kind = rows_of(t), KIND[t]
                    ps = full("gate", t, j)
                    free(act.activation(xn[kind][0:m, j * BLOCK:(j + 1) * BLOCK], ps[0:m, :], ACT.Sigmoid), "gate", t, j)

            def final(t):
                act.wait_ge(x_gated, t + 1)
                rms(("final", t), t)

            do = {"turn": turn, "gates": gates, "project": project, "weigh": weigh, "turn_qk": turn_qk,
                  "values": values, "state": state_update, "sample_read": sample_read, "heads": heads, "pool": pool,
                  "turn2": turn2, "query": query, "match": match_keys, "choose": choose, "turn3": turn3, "gate": gate,
                  "final": final}
            late = None
            for e in SCHEDULE:
                if e[0] in ("slots", "flush"):
                    if late:
                        weights(*late)
                    late = e[1:]
                elif e[0] in do:
                    do[e[0]](*e[1:])

        @block.vector
        def _(dve):
            after, full, free = reader(dve, vector_step)

            def step(ins):
                after(ins)

            def turn_back(name, t, col):
                m, n = rows_of(t), 1 if KIND[t] == "S" else 2
                c = KT // n
                for i in range(n):
                    ps = full(name, t, i)
                    gains = cols[:, layer_of(t), col + i * c:col + (i + 1) * c]
                    free(dve.tensor_tensor(turned[KIND[t]][:, i * c:(i + 1) * c, :],
                                           ps[:, 0:c * m].rearrange("p (h c) -> p h c", h=c), across(gains, m), ALU.mult),
                         name, t, i)

            def invert(e, t, inv):
                m = rows_of(t)
                dve.wait_ge(root_ready, count(RMS_STAGES, e))
                step(dve.reciprocal(inv[:, 0:1], r_root[0:m, :]))
                after(dve.tensor_scalar(inv[:, 1:2], inv[:, 0:1], HD ** -0.5, None, ALU.mult), inv_ready)

            def turn(t):
                if t == 0:
                    dve.wait_ge(small_in, 16 * 4)
                turn_back("turn", t, 0)
                invert(("turn", t), t, inv1[KIND[t]])

            def gates(t):
                m, kind = rows_of(t), KIND[t]
                ps = full("gates", t)
                free(dve.scalar_tensor_tensor(g8[kind][:, :], ps[0:m, 0:8], inv1[kind][:, 0:1],
                                              b_gates[0:m, layer_of(t), :], ALU.mult, ALU.add), "gates", t)
                after(dve.scalar_tensor_tensor(ga[0:m, :], g8[kind][:, 4:8], -1.0, g8[kind][:, 4:8], ALU.mult, ALU.max), gate_abs)
                dve.wait_ge(gate_ln, t + 1)
                after(dve.scalar_tensor_tensor(lf[kind][:, :], g8[kind][:, 4:8], 0.0, gc[0:m, :], ALU.min, ALU.subtract),
                      lf_ready)

            def cumulate(t):
                ps = full("cum", t)
                free(dve.tensor_copy(mb[:, 4:8], ps[:, 0:4]), "cum", t)
                step(dve.tensor_tensor(lead[:, :], g8["A"][:, 0:4], mb[:, 4:8], ALU.subtract))
                after(dve.tensor_tensor(prod[:, :, :], down(const("ident"), HEADS), across(lead[:, :], P), ALU.mult),
                      lead_diag)

            def spread(t):
                ps = full("spread", t)
                free(dve.tensor_tensor(decayed[:, :, :], heads_view(ps[:, :], P), down(const("mask"), HEADS), ALU.add),
                     "spread", t)
                step(dve.tensor_reduce(neg_m[:, :], decayed[:, :, :], AX.X, ALU.max))
                if KIND[t] == "A":
                    step(dve.tensor_scalar(mb[:, 0:4], neg_m[:, :], 0.0, None, ALU.max))
                else:
                    step(dve.tensor_tensor(mb[:, 0:4], neg_m[:, :], m_prev[:, :], ALU.max))
                after(dve.tensor_scalar(neg_m[:, :], mb[:, 0:4], -1.0, None, ALU.mult), decay_args)

            def weigh(t):
                if KIND[t] == "A":
                    step(dve.tensor_copy(args1[:, 0:4], neg_m[:, :]))
                else:
                    step(dve.tensor_tensor(args1[:, 0:4], m_prev[:, :], mb[:, 0:4], ALU.subtract))
                after(dve.tensor_tensor(args1[:, 4:8], neg_m[:, :], mb[:, 4:8], ALU.subtract), args1_ready)

            def scores(t):
                dve.wait_ge(decay_done, count(("weigh",), ("weigh", t)))
                ps = full("scores", t)
                free(dve.tensor_tensor(prod[:, :, :], heads_view(ps[:, :], P), decayed[:, :, :], ALU.mult), "scores", t)

            def values(t):
                if KIND[t] == "B":
                    emptied(dve, "inter", t, 0)
                    emptied(dve, "inter", t, 1)
                for i in range(2):
                    ps = full("values", t, i)
                    two = ps[:, 0:258].rearrange("p (h e) -> p h e", h=2)
                    dst = num[:, 2 * i:2 * i + 2, :]
                    if KIND[t] == "B":
                        ins = dve.tensor_tensor(dst, two, inter[:, 2 * i:2 * i + 2, :], ALU.add)
                    else:
                        ins = dve.tensor_copy(dst, two)
                    free(ins, "values", t, i)

            def state_update(t):
                n, kind = count(("state",), ("state", t)), KIND[t]
                ps = full("last", t)
                free(dve.tensor_copy(last[:, :], ps[:, 0:8]), "last", t)
                step(dve.tensor_tensor(args2[:, 0:4], lead[:, :], last[:, 0:4], ALU.subtract))
                if kind == "A":
                    if t:
                        dve.wait_ge(prompt_stored, 48)
                    after(dve.tensor_scalar(args2[:, 4:8], last[:, 0:4], -1.0, None, ALU.mult), args2_ready)
                else:
                    after(dve.tensor_tensor(args2[:, 4:8], m_prev[:, :], last[:, 0:4], ALU.subtract), args2_ready)
                step(dve.tensor_tensor(m_prev[:, :], last[:, 0:4], last[:, 4:8], ALU.add))
                dve.wait_ge(exps2_ready, n)
                emptied(dve, "project", t, 1)
                after(dve.tensor_tensor(prod[:, :, :], heads_view(k["A"][:, :], P), across(exps2[:, 0:4], P), ALU.mult),
                      k_weighted)
                for i in range(2):
                    ps = full("state", t, i)
                    if kind == "A":
                        ins = dve.tensor_copy(state[:, 2 * i:2 * i + 2, :], ps[:, 0:258].rearrange("p (h e) -> p h e", h=2))
                    else:
                        for h in range(2):
                            hh = 2 * i + h
                            ins = dve.scalar_tensor_tensor(state[:, hh, :], state[:, hh, :], exps2[:, 4 + hh:5 + hh],
                                                           ps[:, h * 129:h * 129 + 129], ALU.mult, ALU.add)
                            if h == 0:
                                step(ins)
                    free(ins, "state", t, i)
                after(dve.tensor_copy(den[0:1, 0:1], state[0:1, 0, 0:1]), state_written)

            def sample_read(t):
                n, layer = layer_of(t) + 1, layer_of(t)
                ig = g8["S"][:, 0:4]
                if layer:
                    dve.wait_ge(samples_stored, 48)
                step(dve.tensor_tensor(args1[0:DEC, 0:4], lf["S"][:, :], m_s[:, layer, :], ALU.add))
                step(dve.tensor_tensor(m_s_new[:, :], ig, args1[0:DEC, 0:4], ALU.max))
                step(dve.tensor_tensor(args1[0:DEC, 0:4], args1[0:DEC, 0:4], m_s_new[:, :], ALU.subtract))
                step(dve.tensor_tensor(args1[0:DEC, 4:8], ig, m_s_new[:, :], ALU.subtract))
                after(dve.tensor_scalar(args1[0:DEC, 8:12], m_s_new[:, :], -1.0, None, ALU.mult), sample_args)
                ps = full("turn_qs", t)
                free(dve.tensor_tensor(
                    q_own[:, :, :, :],
                    ps[:, 0:32].rearrange("p (h b o) -> p h b o", h=HEADS, o=1).to_broadcast([P, HEADS, DEC, DEC]),
                    const("own").rearrange("p (o b j) -> p o b j", o=1, b=DEC).to_broadcast([P, HEADS, DEC, DEC]),
                    ALU.mult), "turn_qs", t)
                dve.wait_ge(sample_exp, n)
                after(dve.tensor_tensor(w_own[:, :, :], const("own_head", DEC).rearrange("p (b h) -> p b h", b=DEC),
                                        down(exps1[0:DEC, 0:4], DEC), ALU.mult), w_own_ready)
                emptied(dve, "project", t, 0)
                emptied(dve, "project", t, 1)
                emptied(dve, "project", t, 2)
                s512 = junk[0:DEC, :, :]
                step(dve.tensor_tensor(s512, heads_view(q["S"][:, :], DEC), heads_view(k["S"][:, :], DEC), ALU.mult))
                step(dve.tensor_reduce(qk_s[:, :], s512, AX.X, ALU.add))
                step(dve.tensor_tensor(qk_s[:, :], qk_s[:, :], exps1[0:DEC, 4:8], ALU.mult))
                step(dve.tensor_tensor(inter[0:DEC, :, :], v["S"][:, :, :], across(qk_s[:, :], HD + 1), ALU.mult))
                step(dve.tensor_tensor(heads_view(k["S"][:, :], DEC), heads_view(k["S"][:, :], DEC),
                                       across(exps1[0:DEC, 4:8], HD), ALU.mult))
                ps = full("w_spread", t)
                free(dve.tensor_copy(w_spread[:, :], ps[:, 0:32]), "w_spread", t)
                for i in range(2):
                    ps = full("read", t, i)
                    for h in range(2):
                        hh = 2 * i + h
                        ins = dve.scalar_tensor_tensor(num[0:DEC, hh, :], ps[0:DEC, h * 129:h * 129 + 129],
                                                       exps1[0:DEC, hh:hh + 1], inter[0:DEC, hh, :], ALU.mult, ALU.add)
                        if h == 0:
                            step(ins)
                    free(ins, "read", t, i)

            def sample_k_own(t, b):
                after(dve.tensor_scalar(pq[0:DEC, b % 2, :], k["S"][:, :], const("ident", DEC)[:, b:b + 1], None, ALU.mult),
                      sample_k)

            def sample_write(t, b):
                if b == 0:
                    sample_k_own(t, 0)
                if b + 1 < DEC:
                    sample_k_own(t, b + 1)
                for i in range(2):
                    ps = full("write", t, b, i)
                    for h in range(2):
                        s = b * HEADS + 2 * i + h
                        ins = dve.scalar_tensor_tensor(cs[:, s, :], cs[:, s, :], w_spread[:, s:s + 1],
                                                       ps[:, h * 129:h * 129 + 129], ALU.mult, ALU.add)
                        if h == 0:
                            step(ins)
                    free(ins, "write", t, b, i)
                if b == DEC - 1:
                    after(dve.tensor_copy(den[0:1, 0:1], cs[0:1, 0, 0:1]), sample_state)

            def heads(t):
                m, kind = rows_of(t), KIND[t]
                if kind == "S":
                    floor = exps1[0:m, 8:12]
                else:
                    dve.wait_ge(exps1_ready, count(("weigh",), ("weigh", t)))
                    floor = exps1[:, 4:8]
                n3 = num[0:m, :, 0:HD]
                o3 = heads_view(o[kind][:, :], m)
                total = num[0:m, :, HD:HD + 1].rearrange("p h o -> p (h o)")
                step(dve.scalar_tensor_tensor(den[0:m, :], total, -1.0, total, ALU.mult, ALU.max))
                step(dve.tensor_tensor(den[0:m, :], den[0:m, :], floor, ALU.max))
                step(dve.reciprocal(den[0:m, :], den[0:m, :]))
                step(dve.tensor_tensor(n3, n3, across(den[0:m, :], HD), ALU.mult))
                step(dve.tensor_tensor(junk[0:m, :, :], n3, n3, ALU.mult))
                after(dve.tensor_reduce(h_in[0:m, :], junk[0:m, :, :], AX.X, ALU.add), head_var)
                emptied(dve, "project", t, 3)
                step(dve.tensor_tensor(n3, n3, o3, ALU.mult))
                dve.wait_ge(head_root, t + 1)
                step(dve.reciprocal(h_inv[0:m, :], h_root[0:m, :]))
                after(dve.tensor_tensor(n3, n3, across(h_inv[0:m, :], HD), ALU.mult), heads_ready)
                ps = full("heads", t)
                free(dve.tensor_tensor(turned[kind][:, 0:4, :], heads_view(ps[:, 0:4 * m], m),
                                       across(cols[:, layer_of(t), 16:20], m), ALU.mult), "heads", t)

            def pool(t):
                m = rows_of(t)
                ps = full("pool_z", t)
                free(dve.tensor_tensor(turned[KIND[t]][:, 4:8, :], heads_view(ps[:, 0:4 * m], m),
                                       across(cols[:, layer_of(t), 20:24], m), ALU.mult), "pool_z", t)

            def mix(p, j, h):
                if h == 0:
                    return
                for t in PASS_TILES[p]:
                    m = rows_of(t)
                    part = x[KIND[t]][:, j * BLOCK:(j + 1) * BLOCK]
                    free(dve.tensor_tensor(part, part, full("mix", t, j)[0:m, :], ALU.add), "mix", t, j)

            def turn2(t):
                kind = KIND[t]
                turn_back("turn2", t, 8)
                invert(("turn2", t), t, inv2[kind])
                dve.wait_ge(layer_in, 48 * (layer_of(t) + 1))
                if kind != "S":
                    step(dve.scalar_tensor_tensor(xn[kind][:, :], x[kind][:, :], inv2[kind][:, 0:1], gain2[:, :],
                                                  ALU.mult, ALU.mult))
                    return
                after(dve.memset(pqT_s, 0.0), zeros_set)
                ps = full("rep_inv", t)
                free(dve.tensor_copy(inv_rep[:, :], ps[0:64, 0:1]), "rep_inv", t)
                for i in range(2):
                    lo = i * BLOCK
                    ps = full("rep", t, i)
                    free(dve.scalar_tensor_tensor(xn[kind][:, lo:lo + BLOCK], ps[0:64, :], inv_rep[:, 0:1],
                                                  gain2[0:64, lo:lo + BLOCK], ALU.mult, ALU.mult), "rep", t, i)

            def top16(values, idx, src):
                step(dve.max(values[:, 0:8], src))
                step(dve.max_index(idx[:, 0:8], values[:, 0:8], src))
                step(dve.match_replace(src, values[:, 0:8], src, REMOVED))
                step(dve.max(values[:, 8:16], src))
                step(dve.max_index(idx[:, 8:16], values[:, 8:16], src))

            def rank(t, i):
                if KIND[t] == "S":
                    emptied(dve, "match", t, 3)
                    top16(top[:, 0, :], top_i[:, 0, :], match_s)
                    return
                emptied(dve, "match", t, i // 4)
                top16(top[:, i, :], top_i[:, i, :], match[:, i * P:(i + 1) * P])

            def pairs(t):
                kind, first = KIND[t], float(layer_of(t) * EXPERTS)
                if kind == "S":
                    m, hs = PH * DEC, 1
                    after(dve.tensor_copy(top_f[:, 0, :], top_i[:, 0, :]), pair_src)
                    ps = full("pairs", t)
                    free(dve.tensor_copy(pair_s[:, :, :], ps[0:64, 0:64].rearrange("p (c k) -> p c k", c=4)), "pairs", t)
                    v0, i0, v1, i1 = (pair_s[:, c:c + 1, :] for c in range(4))
                else:
                    m, hs = P, PH
                    step(dve.tensor_copy(top_f[:, :, :], top_i[:, :, :]))
                    vals = top[:, :, :].rearrange("p (h c) k -> p h c k", c=2)
                    inds = top_f[:, :, :].rearrange("p (h c) k -> p h c k", c=2)
                    v0, v1, i0, i1 = vals[:, :, 0, :], vals[:, :, 1, :], inds[:, :, 0, :], inds[:, :, 1, :]
                b0 = base[0:m, 0:hs, :]
                step(dve.tensor_scalar(b0, i0, float(NKEYS), first, ALU.mult, ALU.add))
                for dst, s0, s1 in ((sums, v0, v1), (codes, b0, i1)):
                    at = 0
                    for r in range(TOPK // 2):
                        n = STAIR[r]
                        dve.tensor_tensor(dst[0:m, 0:hs, at:at + n], s0[:, :, r:r + 1].to_broadcast([m, hs, n]),
                                          s1[:, :, 0:n], ALU.add)
                        at += n
                    n = TOPK // 2
                    step(dve.tensor_tensor(dst[0:m, 0:hs, at:at + n], s0[:, :, n:2 * n],
                                           s1[:, :, 0:1].to_broadcast([m, hs, n]), ALU.add))

            def find_best(t, h):
                m = LANES[KIND[t]]
                top16(best[0:m, h, :], best_i[0:m, h, :], sums[0:m, h, :])
                step(dve.tensor_copy(best_f[0:m, h, :], best_i[0:m, h, :]))
                shape = [m, TOPK, CANDS]
                hot = onehot[0:m, :, :]
                step(dve.tensor_tensor(hot, down(const("place", m), TOPK), across(best_f[0:m, h, :], CANDS), ALU.is_equal))
                step(dve.tensor_tensor(hot, hot, down(codes[0:m, h, :], TOPK), ALU.mult))
                step(dve.tensor_reduce(chosen[0:m, h, :], hot, AX.X, ALU.add))

            def choose(t):
                kind = KIND[t]
                m, hs = LANES[kind], 1 if kind == "S" else PH
                b3 = best[0:m, 0:hs, :]
                hk = [m, hs, TOPK]
                step(dve.tensor_copy(base[0:m, 0:hs, 0:1], best[0:m, 0:hs, 0:1]))
                after(dve.tensor_tensor(b3, b3, base[0:m, 0:hs, 0:1].to_broadcast(hk), ALU.subtract), logits_ready)
                dve.wait_ge(logits_exp, t + 1)
                step(dve.tensor_reduce(shares[0:m, 0:hs], b3, AX.X, ALU.add))
                step(dve.reciprocal(shares[0:m, 0:hs], shares[0:m, 0:hs]))
                step(dve.tensor_tensor(prob[kind][:, :].rearrange("p (h k) -> p h k", h=hs), b3,
                                       across(shares[0:m, 0:hs], TOPK), ALU.mult))
                after(dve.tensor_copy(index[kind][:, :].rearrange("p (h k) -> p h k", h=hs), chosen[0:m, 0:hs, :]),
                      index_ready)

            def take_dots(t, g):
                kind = KIND[t]
                lanes = LANES[kind]
                for i in range(GROUP):
                    n = FIRST_SLOT[t] + g * GROUP + i
                    dve.wait_ge(row_in[n % RING], 16 * (n // RING + 1))
                    u = rows[0:lanes, n % RING, 0:D]
                    s = g * GROUP + i
                    ins = dve.scalar_tensor_tensor(u, u, 1.0, xn[kind][:, :], ALU.mult, ALU.mult,
                                                   accum_out=dots[kind][:, s:s + 1])
                ins.then_inc(dot_done, 1)

            def weights(t, g):
                lanes, n = LANES[KIND[t]], FIRST_SLOT[t] // GROUP + g
                dve.wait_ge(gelu_done, n + 1)
                after(dve.tensor_tensor(wts[0:lanes, n % 4, :], gel[0:lanes, n % 4, :],
                                        prob[KIND[t]][:, g * GROUP:(g + 1) * GROUP], ALU.mult), weight_done)

            def add_experts(t):
                kind = KIND[t]
                m = ROWS[kind]
                dve.wait_ge(slot_used, FIRST_SLOT[t] + SLOTS[kind])
                after(dve.tensor_tensor(x[kind][:, :], x[kind][:, :], acc[0:m, :, :].rearrange("p c n -> p (c n)"), ALU.add),
                      acc_read)

            def embed(p):
                for t in PASS_TILES[p]:
                    m, kind = rows_of(t), KIND[t]
                    for j in range(2):
                        emptied(dve, "gate", t, j)
                        ps = full("embed", t, j)
                        sig = xn[kind][0:m, j * BLOCK:(j + 1) * BLOCK]
                        free(dve.tensor_tensor(sig, sig, ps[0:m, :], ALU.mult), "embed", t, j)
                    after(dve.tensor_tensor(x[kind][:, :], x[kind][:, :], xn[kind][0:m, :], ALU.add), x_gated)

            def final(t):
                kind = KIND[t]
                invert(("final", t), t, inv2[kind])
                dve.wait_ge(layer_in, 16 * (3 * DEPTH + 1))
                after(dve.scalar_tensor_tensor(x[kind][:, :], x[kind][:, :], inv2[kind][:, 0:1], gain2[0:rows_of(t), :],
                                               ALU.mult, ALU.mult), x_final)

            dve.memset(v["A"][:, :, HD:HD + 1], 1.0)
            after(dve.memset(v["S"][:, :, HD:HD + 1], 1.0), ones_set)

            do = {"turn": turn, "gates": gates, "cum": cumulate, "spread": spread, "weigh": weigh, "scores": scores,
                  "values": values, "state": state_update, "sample_read": sample_read, "sample_write": sample_write,
                  "heads": heads, "pool": pool, "mix": mix, "turn2": turn2, "rank": rank, "pairs": pairs,
                  "best": find_best, "choose": choose, "embed": embed, "final": final}
            late = older = None
            for e in SCHEDULE:
                if e[0] in ("slots", "flush"):
                    if e[0] == "slots":
                        take_dots(*e[1:])
                    if late:
                        weights(*late)
                    if older and older[1] == SLOTS[KIND[older[0]]] // GROUP - 1:
                        add_experts(older[0])
                    older, late = late, e[1:]
                    if e[0] == "flush":
                        add_experts(older[0])
                elif e[0] in do:
                    do[e[0]](*e[1:])


def shape_constants():
    c = {n: np.zeros((P, w), np.float32) for n, w in _widths}
    r = np.arange(P)
    c["ident"][:] = np.eye(P)
    c["tri"][:] = r[:, None] <= r[None, :]
    c["mask"][:] = np.where(r[None, :] <= r[:, None], 0.0, NEG)
    c["ones"][:] = 1.0
    for g, w in enumerate(WINDOWS):
        s, t = r[:, None], r[None, :]
        inside = (s <= t) & (s > t - w)
        cols = slice(g * P, (g + 1) * P)
        c["band_a"][:, cols] = inside / np.minimum(t + 1, w) - np.eye(P)
        c["band_b"][:, cols] = inside / w - np.eye(P)
        c["band_prev"][:, cols] = ((s - P > t - w)) / w
        for b in range(DEC):
            c["band_buf"][b * TAIL + TAIL - (w - 1):(b + 1) * TAIL, g * 8 + b] = 1.0 / w
            c["band_new"][b, g * 8 + b] = 1.0 / w - 1.0
    for b in range(DEC):
        c["own"][:, b * DEC + b] = 1.0
        c["own_head"][b, b * HEADS:(b + 1) * HEADS] = 1.0
        for h in range(PH):
            for half in range(2):
                c[f"key{half}"][(2 * h + half) * DEC + b, h * DEC + b] = 1.0
            c["copy8"][b, h * DEC + b] = 1.0
            c["own_token"][h * DEC + b, b] = 1.0
    c["place"][:] = np.arange(CANDS)
    c["eps"][:] = EPS
    return np.concatenate([c[n] for n, _ in _widths], axis=1)


OUTS = {"out_y": (SEQ + DEC, D), "out_c_p": (DEPTH, P, HEADS * (HD + 1)), "out_m_p": (DEPTH, HEADS),
        "out_pool_p": (DEPTH, TAIL, POOLW), "out_c_s": (DEPTH, P, DEC * HEADS * (HD + 1)),
        "out_m_s": (DEPTH, DEC, HEADS), "out_pool_s": (DEPTH, DEC, TAIL, POOLW)}


def layout(i):
    f = {n: np.asarray(z) for n, z in i.items()}

    def halves(w):
        n = w.shape[2] // BLOCK
        return w.reshape(DEPTH, 2, 4, P, n, BLOCK).transpose(0, 4, 1, 3, 2, 5).reshape(DEPTH, 2 * n, P, 4 * BLOCK)

    w_in = f["w_in"]
    dense_in, gates_in = w_in[:, :, :2560], w_in[:, :, 2560:]
    ple = f["w_ple"].reshape(DEPTH, 1, 2, P, 2, BLOCK).transpose(0, 1, 3, 4, 2, 5).reshape(DEPTH, 1, P, 4 * BLOCK)
    emb = np.concatenate([f["p_prompt"][:, 0], f["p_sample"][:, :, 0]], axis=1)

    def column(name, n):
        return f[name].reshape(DEPTH, n, P).transpose(2, 0, 1)

    c_n = np.concatenate([f["state_C"], f["state_n"][..., None]], axis=-1)
    return {
        "x": np.concatenate([f["x_prompt"][0], f["x_sample"][:, 0]], axis=0),
        "consts": shape_constants(),
        "w": np.concatenate([halves(dense_in), halves(f["w_out"]), halves(f["peer_wq"]), halves(f["w_gate"]), ple], axis=1),
        "w_gates": gates_in.reshape(DEPTH, KT, P, 8).transpose(2, 0, 1, 3).reshape(P, -1),
        "b_gates": np.broadcast_to(f["b_gate"].reshape(1, -1), (P, DEPTH * 8)),
        "cols": np.concatenate([column("norm1", 8), column("norm2", 8), column("mlstm_norm", 4), column("pool_scale", 4)],
                               axis=2).reshape(P, -1),
        "w_pool": f["w_pool"].transpose(0, 2, 1, 3).reshape(DEPTH, P, -1),
        "emb": emb.reshape(DEPTH, SEQ + DEC, 2, P).transpose(0, 3, 2, 1),
        "m_s": f["state_m"].transpose(1, 0, 2).reshape(DEC, -1),
        "keys": f["peer_keys"].transpose(0, 4, 2, 1, 3).reshape(DEPTH, P, -1),
        "gain": np.broadcast_to(np.concatenate([f["norm2"], f["norm_f"][None]])[:, None], (DEPTH + 1, P, D)),
        "c_s": c_n.transpose(0, 3, 1, 2, 4).reshape(DEPTH, P, -1),
        "pool_buf": f["state_pool"].reshape(DEPTH, DEC * TAIL, POOLW),
        "pool_old": f["state_pool"],
        "uv": np.concatenate([f["peer_u"], f["peer_v"]], axis=2).reshape(DEPTH * EXPERTS, 2 * D),
    }


def kernel(**inputs):
    import concourse.bacc as bacc
    from concourse.bass_utils import run_bass_kernel_spmd

    nc = bacc.Bacc("TRN2", target_bir_lowering=False, num_devices=1)
    arrays, a = {}, {}
    for name, z in layout(inputs).items():
        arrays[f"in_{name}"] = np.ascontiguousarray(z)
        a[name] = nc.dram_tensor(f"in_{name}", z.shape, F32, kind="ExternalInput").ap()
    for name, shape in OUTS.items():
        a[name] = nc.dram_tensor(name, shape, F32, kind="ExternalOutput").ap()
    build(nc, a)
    r = run_bass_kernel_spmd(nc, [arrays], core_ids=[0]).results[0]
    y = r["out_y"]
    c_p = r["out_c_p"].reshape(DEPTH, HD, 1, HEADS, HD + 1).transpose(0, 2, 3, 1, 4)
    c_s = r["out_c_s"].reshape(DEPTH, HD, DEC, HEADS, HD + 1).transpose(0, 2, 3, 1, 4)
    return (y[:SEQ].reshape(1, SEQ, D), y[SEQ:].reshape(DEC, 1, D),
            np.ascontiguousarray(c_p[..., :HD]), np.ascontiguousarray(c_p[..., HD]),
            r["out_m_p"].reshape(DEPTH, 1, HEADS), r["out_pool_p"].reshape(DEPTH, 1, TAIL, POOLW),
            np.ascontiguousarray(c_s[..., :HD]), np.ascontiguousarray(c_s[..., HD]),
            r["out_m_s"], r["out_pool_s"])
```

```python
from contextlib import ExitStack

import concourse.bass as bass
import numpy as np
from concourse import mybir

F32 = mybir.dt.float32
U32 = mybir.dt.uint32
ALU = mybir.AluOpType
ACT = mybir.ActivationFunctionType
AX = mybir.AxisListType.X

DEPTH, SEQ, DEC, D = 2, 256, 8, 1024
HEADS, HD, POOLW = 4, 128, 512
WINDOWS = (2, 4, 8, 16)
TAIL = max(WINDOWS) - 1
PH, NKEYS, EXPERTS, TOPK = 8, 128, 16384, 16
PLE = 256
EPS = 1e-6
P = 128
KT = D // P
BLOCK = 512
IN0, OUT0, PQ0, GATE0, PLE0, HALVES = 0, 10, 14, 22, 26, 27
PAIRS = PH * TOPK
STAIR = [TOPK // (a + 1) for a in range(TOPK)]
CANDS = sum(STAIR)
NEG = -1e30
REMOVED = -3e38

EARLY = 15
RING = 8
GROUP = 2
DIAGS = 2
WRING = 3
BANKS = 6

_widths = [("ident", P), ("tri", P), ("mask", P), ("ones", P), ("band_a", 4 * P), ("band_b", 4 * P),
           ("band_prev", 4 * P), ("band_buf", 32), ("band_new", 32), ("own", 64), ("own_head", 32), ("key0", 64),
           ("key1", 64), ("copy8", 64), ("own_token", 8), ("place", CANDS), ("eps", 1)]
AT, _at = {}, 0
for _name, _w in _widths:
    AT[_name] = (_at, _w)
    _at += _w
NCONST = _at

KIND = ["A", "B", "S", "A", "B", "S"]
PASS_TILES = [[0], [1, 2], [3], [4, 5]]
ROWS = {"A": P, "B": P, "S": DEC}
LANES = {"A": P, "B": P, "S": PH * DEC}
SLOTS = {"A": PAIRS, "B": PAIRS, "S": TOPK}


COST = {"layer": 0.0, "turn": 3.5, "gates": 3.0, "project": 3, "cum": 2.5, "spread": 3.5, "weigh": 2.5,
        "turn_qk": 3.0, "scores": 3.0, "values": 2, "state": 3.5, "heads": 2.5, "sample_read": 5.5,
        "sample_write": 2.25, "pool": 2, "mix": 3.5, "turn2": 4.5, "query": 3.5, "match": 1.5, "rank": 2.05,
        "pairs": 3.75, "best": 6.5, "choose": 3.5, "turn3": 3.0, "gate": 4.0, "embed": 6.0, "final": 4.0,
        "turn_prod": 2, "state_args": 3, "norm_heads": 3.5, "pool_r": 2, "turn_pq": 1.5, "weigh_keys": 1.5}


def layer_of(tile):
    return tile // 3


def stage_front(p):
    tiles = PASS_TILES[p]
    big, small = tiles[0], tiles[1:]
    out = []

    def add(stage, *key):
        out.append((stage, *key))

    if p % 2 == 0:
        add("layer", layer_of(big))
    for t in tiles:
        add("turn", t)
    for t in tiles:
        add("gates", t)
    extra = {1: ["cum"], 2: ["spread", "turn_qk"], 3: ["weigh", "scores"], 4: ["turn_prod", "values"]}
    for j in range(5):
        for h in range(2):
            for t in tiles:
                add("project", p, j, h, t)
        for s in extra.get(j, []):
            add(s, big)
    if p:
        add("state_args", big)
    add("norm_heads", big)
    if p:
        add("weigh_keys", big)
    else:
        add("pool_r", big)
        add("pool", big)
    add("heads", big)
    if p:
        add("state", big)
    for t in small:
        add("sample_read", t)
        for b in range(DEC):
            add("sample_write", t, b)
        add("norm_heads", t)
        add("heads", t)
    for t in tiles if p else []:
        add("pool_r", t)
    for t in tiles if p else []:
        add("pool", t)
    for j in range(2):
        for h in range(2):
            for t in tiles:
                add("mix", p, j, h, t)
    for t in tiles:
        add("turn2", t)
    for j in range(4):
        for h in range(2):
            for t in tiles:
                add("query", p, j, h, t)
        if (p, j) == (0, 1):
            add("state_args", big)
        for t in tiles:
            add("turn_pq", t, j)
        if (p, j) == (0, 1):
            add("weigh_keys", big)
        for t in tiles:
            add("match", t, j)
        if (p, j) == (0, 1):
            add("state", big)
        for i in range(4):
            add("rank", big, 4 * j + i)
            first = p == 0 and j == 0
            step = 1 if first else 2
            if (i + 1) % (2 * step) == 0:
                h = (4 * j + i + 1) // 2 - step
                add("pairs", big, h, h + step)
                for one in range(h, h + step):
                    add("best", big, one)
                if p == 0:
                    add("choose", big, h, h + step)
    if p:
        add("choose", big, 0, PH)
    for t in small:
        add("rank", t, 0)
        add("pairs", t, 0, 1)
        add("best", t, 0)
        add("choose", t, 0, 1)
    if p == 0:
        for h in range(2):
            entry = ("query", 0, 1, h, big)
            out.remove(entry)
            out.insert(out.index(("rank", big, 0)), entry)
    return out


def stage_back(p):
    tiles = PASS_TILES[p]
    out = []
    for t in tiles:
        out.append(("turn3", t))
    for h in range(4):
        for t in tiles:
            out.append(("gate", p, h // 2, h % 2, t))
    out.append(("embed", p))
    if layer_of(tiles[0]) == DEPTH - 1:
        for t in tiles:
            out.append(("final", t))
    return out


def groups_of(p):
    return [("slots", t, g) for t in PASS_TILES[p] for g in range(SLOTS[KIND[t]] // GROUP)]


def woven(groups, stages):
    total, done, at, out = sum(COST[s[0]] for s in stages) or 1, 0, 0, []
    room = [0.15 if KIND[g[1]] == "S" else 1 for g in groups]
    for i, g in enumerate(groups):
        out.append(g)
        while i and at < len(stages) and done < total * sum(room[:i + 1]) / (sum(room) - 1):
            done += COST[stages[at][0]]
            out.append(stages[at])
            at += 1
    return out + stages[at:]


def make_schedule():
    first = stage_front(0)
    ready = 1 + first.index(("choose", 0, 0, 1))
    out = first[:ready]
    out += woven(groups_of(0)[:EARLY], first[ready:])
    out += woven(groups_of(0)[EARLY:], stage_front(1))
    out += woven(groups_of(1), stage_back(0) + stage_front(2))
    out += woven(groups_of(2), stage_back(1) + stage_front(3))
    out += woven(groups_of(3), stage_back(2))
    out += [("flush",)] + stage_back(3)
    return out


SCHEDULE = make_schedule()


def count(stages, entry):
    n = 0
    for e in SCHEDULE:
        n += e[0] in stages
        if e == entry:
            return n
    raise KeyError(entry)


def chosen_by(tile, head):
    return next(count(("choose",), e) for e in SCHEDULE if e[:2] == ("choose", tile) and e[2] <= head < e[3])


def last_chosen(tile):
    return chosen_by(tile, (1 if KIND[tile] == "S" else PH) - 1)


def busy_groups():
    out, last = set(), None
    for e in SCHEDULE:
        if e[0] == "slots":
            if last in VECTOR_STAGES:
                out.add(e[1:])
            before, last = e[1:], None
        elif e[0] in VECTOR_STAGES:
            last = e[0]
    return out


VECTOR_STAGES = ("rank", "pairs", "best", "choose", "norm_heads", "state", "embed")
BUSY = busy_groups()


def on_tensor(tile, slot):
    if KIND[tile] == "S":
        return slot % 2 == 0 or slot == TOPK - 1
    return slot % 2 == 0 or (tile, slot // GROUP) in BUSY


def carried(tile, slot):
    return KIND[tile] == "S" and slot % 2 == 1


RMS_STAGES = ("turn", "turn2", "final")

FIRST_SLOT = {}
_n = 0
for _p in range(4):
    for _t in PASS_TILES[_p]:
        FIRST_SLOT[_t] = _n
        _n += SLOTS[KIND[_t]]
TENSOR_ADDED, VECTOR_ADDED, SLOT_OF = [], [], []
for _t in range(6):
    for _s in range(SLOTS[KIND[_t]]):
        _own = on_tensor(_t, _s)
        SLOT_OF.append((_t, _s))
        TENSOR_ADDED.append((TENSOR_ADDED or [0])[-1] + _own)
        VECTOR_ADDED.append((VECTOR_ADDED or [0])[-1] + (not _own))

HALF_OF = {}
for _e in SCHEDULE:
    if _e[0] in ("project", "mix", "query", "gate", "embed"):
        HALF_OF.setdefault(_e[:4], len(HALF_OF))
HALVES_IN_ORDER = list(HALF_OF)


def half_index(e):
    if e[0] == "embed":
        return PLE0
    return {"project": IN0, "mix": OUT0, "query": PQ0, "gate": GATE0}[e[0]] + 2 * e[2] + e[3]


def build(nc, a):
    with ExitStack() as ctx:
        def sb(name, *shape, dt=F32):
            return ctx.enter_context(nc.sbuf_tensor(name, list(shape), dt))

        def sem(name):
            return ctx.enter_context(nc.semaphore(name))

        consts = sb("consts", P, NCONST)

        def const(name, rows=P):
            lo, w = AT[name]
            return consts[0:rows, lo:lo + w]

        x = {"A": sb("x_a", P, D), "B": sb("x_b", P, D), "S": sb("x_s", DEC, D)}
        xn = {"A": sb("xn_a", P, D), "B": sb("xn_b", P, D), "S": sb("xn_s", PH * DEC, D)}
        turned = {"A": sb("turned", P, KT, P), "S": sb("turned_s", P, KT, DEC)}
        wring = sb("wring", P, WRING, 4, BLOCK)
        rows = sb("rows", P, RING, 2 * D)
        gain2 = sb("gain2", P, D)
        keys = sb("keys", P, 2 * PH, NKEYS)
        w_gates = sb("w_gates", P, DEPTH, KT, 8)
        b_gates = sb("b_gates", P, DEPTH, 8)
        w_pool = sb("w_pool", P, 4, P)
        cols = sb("cols", P, DEPTH, 24)
        emb = sb("emb", P, 2, P + DEC)
        qk = sb("qk", P, 2, 512)
        q = {"A": qk[:, 0, :], "S": sb("q_s", DEC, 512)}
        k = {"A": qk[:, 1, :], "S": sb("k_s", DEC, 512)}
        v = {"A": sb("v", P, HEADS, HD + 1), "S": sb("v_s", DEC, HEADS, HD + 1)}
        o = {"A": sb("o", P, 512), "S": sb("o_s", DEC, 512)}
        u_in = {"A": sb("u_a", P, 512), "B": sb("u_b", P, 512), "S": sb("u_s", DEC, 512)}
        inv1 = {"A": sb("inv1", P, 2), "S": sb("inv1_s", DEC, 2)}
        inv2 = {"A": sb("inv2", P, 2), "S": sb("inv2_s", DEC, 2)}
        g8 = {"A": sb("g8", P, 8), "S": sb("g8_s", DEC, 8)}
        lf = {"A": sb("lf", P, 4), "S": sb("lf_s", DEC, 4)}
        for of_kind in (turned, q, k, v, o, inv1, inv2, g8, lf):
            of_kind["B"] = of_kind["A"]
        qT, kT = sb("q_t", P, HEADS, P), sb("k_t", P, HEADS, P)
        decayed = sb("decayed", P, HEADS, P)
        pooled = {"A": decayed, "B": decayed, "S": sb("pooled_s", P, HEADS, DEC)}
        state = sb("state", P, HEADS, HD + 1)
        mixer = sb("mixer", P, 2 * HEADS * HD + 2 * HEADS * (HD + 1))
        prod, junk = (mixer[:, i * 512:(i + 1) * 512].rearrange("p (h c) -> p h c", h=HEADS) for i in range(2))
        inter, num = (mixer[:, 1024 + i * 516:1024 + (i + 1) * 516].rearrange("p (h c) -> p h c", h=HEADS)
                      for i in range(2))
        scratch = sb("scratch", P, DEC * HEADS * (HD + 1))
        cs = scratch[:, :].rearrange("p (s e) -> p s e", e=HD + 1)
        match = scratch[:, 0:2048]
        onehot = scratch[:, 2048:2848].rearrange("p (k c) -> p k c", c=CANDS)
        match_s = scratch[:, 3648:3648 + NKEYS]
        pool_buf = sb("pool_buf", DEC * TAIL, POOLW)
        ga, gb, gc = sb("gate_abs_f", P, 4), sb("gate_exp_f", P, 4), sb("gate_ln_f", P, 4)
        lead = sb("lead", P, 4)
        mb = sb("mb", P, 8)
        neg_m = sb("neg_m", P, 4)
        m_prev = sb("m_prev", P, 4)
        last = sb("last_mb", P, 8)
        args1, exps1 = sb("args1", P, 12), sb("exps1", P, 12)
        args2, exps2 = sb("args2", P, 8), sb("exps2", P, 8)
        w_own = sb("w_own", DEC, DEC, 4)
        w_spread = sb("w_spread", P, 32)
        qk_s = sb("qk_s", DEC, 4)
        m_s = sb("m_s", DEC, DEPTH, 4)
        m_s_new = sb("m_s_new", DEC, 4)
        q_own = sb("q_own", P, HEADS, DEC, DEC)
        den = sb("den", P, 4)
        h_in, h_root, h_inv = sb("h_in", P, 4), sb("h_root", P, 4), sb("h_inv", P, 4)
        r_in, r_root = sb("r_in", P, 1), sb("r_root", P, 1)
        inv_rep = sb("inv_rep", PH * DEC, 1)
        pq, pqT = qk, qT
        pqT_s = mixer[:, 0:2048].rearrange("p (n t) -> p n t", t=P)
        top, top_f = (kT[:, 2 * i:2 * i + 2, :].rearrange("p h (n k) -> p (h n) k", k=TOPK) for i in range(2))
        top_i = sb("top_i", P, 2 * PH, TOPK, dt=U32)
        pair_s = sb("pair_s", PH * DEC, 4, TOPK)
        base, best, best_f, chosen = (decayed[:, i, :].rearrange("p (h k) -> p h k", k=TOPK) for i in range(4))
        sums, codes = (scratch[:, 2848 + i * 400:2848 + (i + 1) * 400].rearrange("p (h c) -> p h c", c=CANDS)
                       for i in range(2))
        best_i = sb("best_i", P, PH, TOPK, dt=U32)
        shares = sb("shares", P, PH)
        index = {t: sb(f"index_{t}", LANES[t], SLOTS[t], dt=U32) for t in "ABS"}
        prob = {t: sb(f"prob_{t}", LANES[t], SLOTS[t]) for t in "ABS"}
        dots = {t: sb(f"dots_{t}", LANES[t], SLOTS[t]) for t in "ABS"}
        gel = sb("gel", P, 4, GROUP)
        wts = sb("wts", P, 4, GROUP)
        diag = sb("diag", P, DIAGS, GROUP, P)

        acc = ctx.enter_context(nc.psum_tensor("acc", [P, 2, BLOCK], F32))
        banks = [ctx.enter_context(nc.psum_tensor(f"bank{i}", [P, BLOCK], F32)) for i in range(BANKS)]

        consts_in, small_in, x_in = sem("consts_in"), sem("small_in"), sem("x_in")
        layer_in, emb_in, states_in = sem("layer_in"), sem("emb_in"), sem("states_in")
        half_in = [sem(f"half_in{i}") for i in range(WRING)]
        row_in = [sem(f"row_in{i}") for i in range(RING)]
        prompt_stored, samples_stored, stored = sem("prompt_stored"), sem("samples_stored"), sem("stored")
        bank_full = [sem(f"bank_full{i}") for i in range(BANKS)]
        bank_free = [sem(f"bank_free{i}") for i in range(BANKS)]
        half_used, slot_used, slot_added = sem("half_used"), sem("slot_used"), sem("slot_added")
        vector_step, scalar_step = sem("vector_step"), sem("scalar_step")
        ones_set, zeros_set = sem("ones_set"), sem("zeros_set")
        inv_ready, gate_abs, lf_ready = sem("inv_ready"), sem("gate_abs"), sem("lf_ready")
        lead_diag, decay_args, args1_ready = sem("lead_diag"), sem("decay_args"), sem("args1_ready")
        args2_ready, k_weighted, state_written = sem("args2_ready"), sem("k_weighted"), sem("state_written")
        head_var, heads_ready = sem("head_var"), sem("heads_ready")
        sample_args, w_own_ready = sem("sample_args"), sem("w_own_ready")
        sample_k, sample_state = sem("sample_k"), sem("sample_state")
        pair_src, logits_ready, index_ready = sem("pair_src"), sem("logits_ready"), sem("index_ready")
        dot_done, weight_done, acc_read = sem("dot_done"), sem("weight_done"), sem("acc_read")
        carry_done = sem("carry_done")
        x_gated, x_final = sem("x_gated"), sem("x_final")
        root_ready, gate_ln, decay_done = sem("root_ready"), sem("gate_ln"), sem("decay_done")
        exps1_ready, exps2_ready, sample_exp = sem("exps1_ready"), sem("exps2_ready"), sem("sample_exp")
        head_root, logits_exp = sem("head_root"), sem("logits_exp")
        gelu_done, diag_done = sem("gelu_done"), sem("diag_done")

        use, uses = {}, []

        def rows_of(t):
            return ROWS[KIND[t]]

        def heads_view(ap, m, n=HEADS):
            return ap.rearrange("p (h c) -> p h c", h=n)

        def across(ap, n):
            m, h = ap.shape
            return ap.rearrange("p (h o) -> p h o", o=1).to_broadcast([m, h, n])

        def down(ap, n):
            m, c = ap.shape
            return ap.rearrange("p (o c) -> p o c", o=1).to_broadcast([m, n, c])

        block = ctx.enter_context(nc.Block())

        def emptied(eng, *name):
            b, n = use[name]
            eng.wait_ge(bank_free[b], n + 1)

        @block.tensor
        def _(pe):
            def opened(*name):
                b, n = len(uses) % BANKS, len(uses) // BANKS
                uses.append(name)
                use[name] = (b, n)
                if n:
                    pe.wait_ge(bank_free[b], n)
                return banks[b]

            def closed(ins, *name):
                ins.then_inc(bank_full[use[name][0]], 1)

            def half(e):
                n = HALF_OF[e]
                pe.wait_ge(half_in[n % WRING], 16 * (n // WRING + 1))
                return wring[:, n % WRING]

            def turn_rows(name, t):
                m, src = rows_of(t), x[KIND[t]]
                n = 1 if KIND[t] == "S" else 2
                for i in range(n):
                    ps = opened(name, t, i)
                    for c in range(KT // n):
                        lo = (i * KT // n + c) * P
                        ins = pe.transpose(ps[:, c * m:(c + 1) * m], src[:, lo:lo + P], const("ident", m)[:, 0:m])
                    closed(ins, name, t, i)

            def dense(name, p, j, h, t, source, parts):
                w, m, kind = half((name, p, j, h)), rows_of(t), KIND[t]
                if h == 0:
                    if j == 0:
                        for s in source:
                            for i in range(1 if kind == "S" or not parts else parts):
                                emptied(pe, *((s, t, i) if parts else (s, t)))
                    ps = opened(name, t, j)
                else:
                    ps = banks[use[(name, t, j)][0]]
                for c in range(4):
                    ins = pe.matmul(ps[0:m, :], turned[kind][:, 4 * h + c, 0:m], w[:, c, :],
                                    start=(h == 0 and c == 0), stop=(h == 1 and c == 3), skip_group_check=True)
                if h == 1:
                    closed(ins, name, t, j)
                elif t == PASS_TILES[p][-1]:
                    ins.then_inc(half_used, 1)

            def turn(t):
                if t == 0:
                    pe.wait_ge(x_in, 48)
                    pe.wait_ge(consts_in, 16)
                if t >= 3:
                    pe.wait_ge(x_gated, t - 2)
                turn_rows("turn", t)

            def gates(t):
                m = rows_of(t)
                if t == 0:
                    pe.wait_ge(small_in, 16 * 4)
                for i in range(1 if KIND[t] == "S" else 2):
                    emptied(pe, "turn", t, i)
                ps = opened("gates", t)
                for c in range(KT):
                    ins = pe.matmul(ps[0:m, 0:8], turned[KIND[t]][:, c, 0:m], w_gates[:, layer_of(t), c, :],
                                    start=(c == 0), stop=(c == KT - 1))
                closed(ins, "gates", t)

            def project(p, j, h, t):
                dense("project", p, j, h, t, ("turn",), 2)

            def cumulate(t):
                pe.wait_ge(lf_ready, t + 1)
                ps = opened("cum", t)
                closed(pe.matmul(ps[:, 0:4], const("tri"), lf["A"][:, :], start=True, stop=True), "cum", t)

            def spread(t):
                pe.wait_ge(lead_diag, count(("cum",), ("cum", t)))
                ps = opened("spread", t)
                closed(pe.matmul(ps[:, :], const("ones"), prod[:, :, :].rearrange("p h s -> p (h s)"),
                                 start=True, stop=True), "spread", t)

            def turn_qk(t):
                for j, name, src in ((0, "turn_q", q["A"]), (1, "turn_k", k["A"])):
                    emptied(pe, "project", t, j)
                    ps = opened(name, t)
                    for h in range(HEADS):
                        ins = pe.transpose(ps[:, h * P:(h + 1) * P], src[:, h * P:(h + 1) * P], const("ident"))
                    closed(ins, name, t)

            def scores(t):
                emptied(pe, "turn_q", t)
                emptied(pe, "turn_k", t)
                ps = opened("scores", t)
                for h in range(HEADS):
                    ins = pe.matmul(ps[:, h * P:(h + 1) * P], qT[:, h, :], kT[:, h, :], start=True, stop=True)
                closed(ins, "scores", t)

            def by_pairs(name, t, lhs, rhs):
                for i in range(2):
                    ps = opened(name, t, i)
                    for h in range(2):
                        ins = pe.matmul(ps[:, h * 129:h * 129 + 129], lhs[:, 2 * i + h, :], rhs[:, 2 * i + h, :],
                                        start=True, stop=True)
                    closed(ins, name, t, i)

            def turn_prod(t):
                emptied(pe, "scores", t)
                ps = opened("turn_prod", t)
                for h in range(HEADS):
                    ins = pe.transpose(ps[:, h * P:(h + 1) * P], prod[:, h, :], const("ident"))
                closed(ins, "turn_prod", t)

            def values(t):
                if KIND[t] == "B":
                    emptied(pe, "state", t - 1, 1)
                    by_pairs("inter", t, qT, state)
                emptied(pe, "turn_prod", t)
                emptied(pe, "project", t, 2)
                by_pairs("values", t, decayed, v["A"])

            def state_args(t):
                pe.wait_ge(decay_args, count(("spread",), ("spread", t)))
                ps = opened("last", t)
                closed(pe.matmul(ps[:, 0:8], const("ident")[:, P - 1:P].to_broadcast([P, P]), mb[:, :], start=True, stop=True), "last", t)

            def state_update(t):
                pe.wait_ge(k_weighted, count(("state",), ("state", t)))
                by_pairs("state", t, prod, v["A"])

            def sample_read(t):
                n = layer_of(t) + 1
                emptied(pe, "project", t, 0)
                ps = opened("turn_qs", t)
                for h in range(HEADS):
                    ins = pe.transpose(ps[:, h * DEC:(h + 1) * DEC], q["S"][:, h * P:(h + 1) * P],
                                       const("ident", DEC)[:, 0:DEC])
                closed(ins, "turn_qs", t)
                pe.wait_ge(w_own_ready, n)
                ps = opened("w_spread", t)
                closed(pe.matmul(ps[:, 0:32], const("ones", DEC), w_own[:, :, :].rearrange("p b h -> p (b h)"),
                                 start=True, stop=True), "w_spread", t)
                emptied(pe, "turn_qs", t)
                pe.wait_ge(states_in, 32 * n)
                for i in range(2):
                    ps = opened("read", t, i)
                    for h in range(2):
                        for b in range(DEC):
                            ins = pe.matmul(ps[0:DEC, h * 129:h * 129 + 129], q_own[:, 2 * i + h, b, :],
                                            cs[:, b * HEADS + 2 * i + h, :], start=(b == 0), stop=(b == DEC - 1))
                    closed(ins, "read", t, i)

            def sample_write(t, b):
                pe.wait_ge(sample_k, count(("sample_write",), ("sample_write", t, b)))
                emptied(pe, "project", t, 2)
                for i in range(2):
                    ps = opened("write", t, b, i)
                    for h in range(2):
                        hh = 2 * i + h
                        ins = pe.matmul(ps[:, h * 129:h * 129 + 129], pq[0:DEC, b % 2, hh * P:(hh + 1) * P],
                                        v["S"][:, hh, :], start=True, stop=True)
                    closed(ins, "write", t, b, i)

            def heads(t):
                m = rows_of(t)
                pe.wait_ge(heads_ready, t + 1)
                ps = opened("heads", t)
                for h in range(HEADS):
                    ins = pe.transpose(ps[:, h * m:(h + 1) * m], num[0:m, h, 0:HD], const("ident", m)[:, 0:m])
                closed(ins, "heads", t)

            def pool_r(t):
                m, kind = rows_of(t), KIND[t]
                emptied(pe, "project", t, 4)
                ps = opened("pool_r", t)
                for g in range(4):
                    out, col = ps[:, g * m:(g + 1) * m], slice(g * P, (g + 1) * P)
                    if kind == "A":
                        ins = pe.matmul(out, u_in["A"][:, col], const("band_a")[:, col], start=True, stop=True)
                    elif kind == "B":
                        pe.matmul(out, u_in["A"][:, col], const("band_prev")[:, col], start=True, stop=False)
                        ins = pe.matmul(out, u_in["B"][:, col], const("band_b")[:, col], start=False, stop=True)
                    else:
                        pe.wait_ge(states_in, 32 * (layer_of(t) + 1))
                        pe.matmul(out, pool_buf[:, col], const("band_buf", DEC * TAIL)[:, g * 8:g * 8 + 8],
                                  start=True, stop=False)
                        ins = pe.matmul(out, u_in["S"][:, col], const("band_new", DEC)[:, g * 8:g * 8 + 8],
                                        start=False, stop=True)
                closed(ins, "pool_r", t)

            def pool(t):
                m = rows_of(t)
                emptied(pe, "pool_r", t)
                pe.wait_ge(layer_in, 48 * (layer_of(t) + 1))
                ps = opened("pool_z", t)
                for g in range(4):
                    ins = pe.matmul(ps[:, g * m:(g + 1) * m], w_pool[:, g, :], pooled[KIND[t]][:, g, 0:m],
                                    start=True, stop=True)
                closed(ins, "pool_z", t)

            def mix(p, j, h, t):
                dense("mix", p, j, h, t, ("heads", "pool_z"), 0)

            def turn2(t):
                emptied(pe, "mix", t, 0)
                emptied(pe, "mix", t, 1)
                turn_rows("turn2", t)
                if KIND[t] == "S":
                    for i in range(2):
                        ps = opened("rep", t, i)
                        closed(pe.matmul(ps[0:64, :], const("copy8", DEC), x["S"][:, i * BLOCK:(i + 1) * BLOCK],
                                         start=True, stop=True), "rep", t, i)
                    pe.wait_ge(inv_ready, count(RMS_STAGES, ("turn2", t)))
                    ps = opened("rep_inv", t)
                    closed(pe.matmul(ps[0:64, 0:2], const("copy8", DEC), inv2["S"][:, :], start=True, stop=True),
                           "rep_inv", t)

            def query(p, j, h, t):
                dense("query", p, j, h, t, ("turn2",), 2)

            def turn_pq(t, j):
                m, kind = rows_of(t), KIND[t]
                emptied(pe, "query", t, j)
                ps = opened("turn_pq", t, j)
                for i in range(4):
                    ins = pe.transpose(ps[:, i * m:(i + 1) * m], pq[0:m, 1 if kind == "S" else 0, i * P:(i + 1) * P],
                                       const("ident", m)[:, 0:m])
                closed(ins, "turn_pq", t, j)

            def match_keys(t, j):
                kind = KIND[t]
                emptied(pe, "turn_pq", t, j)
                if j == 0:
                    pe.wait_ge(layer_in, 48 * (layer_of(t) + 1))
                if kind != "S":
                    ps = opened("match", t, j)
                    for i in range(4):
                        ins = pe.matmul(ps[:, i * P:(i + 1) * P], pqT[:, i, :], keys[:, 4 * j + i, :], start=True, stop=True)
                    closed(ins, "match", t, j)
                elif j == 3:
                    ps = opened("match", t, j)
                    for i in range(2 * PH):
                        ins = pe.matmul(ps[:, 0:P], pqT_s[:, i, :], keys[:, i, :], start=(i == 0), stop=(i == 2 * PH - 1))
                    closed(ins, "match", t, j)

            def pairs(t, h0, h1):
                if KIND[t] != "S":
                    return
                pe.wait_ge(pair_src, layer_of(t) + 1)
                ps = opened("pairs", t)
                for c in range(2):
                    pe.matmul(ps[0:64, c * 32:c * 32 + 16], const(f"key{c}"), top[:, 0, :], start=True, stop=True)
                    ins = pe.matmul(ps[0:64, c * 32 + 16:c * 32 + 32], const(f"key{c}"), top_f[:, 0, :],
                                    start=True, stop=True)
                closed(ins, "pairs", t)

            def add_values(t, g):
                kind = KIND[t]
                m, lanes, n = ROWS[kind], LANES[kind], FIRST_SLOT[t] // GROUP + g
                if g == 0 and t > 0:
                    pe.wait_ge(acc_read, t)
                pe.wait_ge(diag_done, n + 1)
                for i in range(GROUP):
                    s = g * GROUP + i
                    if not on_tensor(t, s):
                        continue
                    ends = s == max(z for z in range(SLOTS[kind]) if on_tensor(t, z))
                    factors = diag[0:lanes, n % DIAGS, i, 0:m]
                    if carried(t, s):
                        pe.wait_ge(carry_done, layer_of(t) + 1)
                        factors = const("own_token", lanes)
                    for c in range(2):
                        lo = D + c * BLOCK
                        ins = pe.matmul(acc[0:m, c, :], factors,
                                        rows[0:lanes, (n * GROUP + i) % RING, lo:lo + BLOCK],
                                        start=(s == 0), stop=ends, skip_group_check=True)
                    ins.then_inc(slot_used, 1)

            def turn3(t):
                pe.wait_ge(acc_read, t + 1)
                turn_rows("turn3", t)

            def gate(p, j, h, t):
                dense("gate", p, j, h, t, ("turn3",), 2)

            def embed(p):
                w = half(("embed", p))
                pe.wait_ge(emb_in, 16 * (p + 1))
                for t in PASS_TILES[p]:
                    m = rows_of(t)
                    lo = P if KIND[t] == "S" else 0
                    for j in range(2):
                        ps = opened("embed", t, j)
                        for c in range(2):
                            ins = pe.matmul(ps[0:m, :], emb[:, c, lo:lo + m], w[:, 2 * j + c, :],
                                            start=(c == 0), stop=(c == 1))
                        closed(ins, "embed", t, j)

            do = {"turn": turn, "gates": gates, "project": project, "cum": cumulate, "spread": spread,
                  "turn_qk": turn_qk, "scores": scores, "turn_prod": turn_prod, "values": values,
                  "state_args": state_args, "state": state_update, "sample_read": sample_read,
                  "sample_write": sample_write, "heads": heads, "pool_r": pool_r, "pool": pool, "mix": mix,
                  "turn2": turn2, "query": query, "turn_pq": turn_pq, "match": match_keys, "pairs": pairs, "turn3": turn3, "gate": gate,
                  "embed": embed}
            late = None
            for e in SCHEDULE:
                if e[0] in ("slots", "flush"):
                    if late:
                        add_values(*late)
                    late = e[1:]
                elif e[0] in do:
                    do[e[0]](*e[1:])

        def reader(eng, step_sem):
            counts = {}

            def after(ins, s=step_sem):
                counts[s.name] = counts.get(s.name, 0) + 1
                ins.then_inc(s, 1)
                eng.wait_ge(s, counts[s.name])

            def full(*name):
                b, n = use[name]
                eng.wait_ge(bank_full[b], n + 1)
                return banks[b]

            def free(ins, *name):
                b, n = use[name]
                ins.then_inc(bank_free[b], 1)
                eng.wait_ge(bank_free[b], n + 1)

            return after, full, free

        @block.sync
        def _(sp):
            sp.dma_start(consts[:, :], a["consts"]).then_inc(consts_in, 16)
            for kind, lo, m in (("A", 0, P), ("B", P, P), ("S", SEQ, DEC)):
                sp.dma_start(x[kind][:, :], a["x"][lo:lo + m, :]).then_inc(x_in, 16)
            sp.dma_start(w_gates[:, :, :, :].rearrange("p l c n -> p (l c n)"), a["w_gates"]).then_inc(small_in, 16)
            sp.dma_start(b_gates[:, :, :].rearrange("p l n -> p (l n)"), a["b_gates"]).then_inc(small_in, 16)
            sp.dma_start(cols[:, :, :].rearrange("p l n -> p (l n)"), a["cols"]).then_inc(small_in, 16)
            sp.dma_start(m_s[:, :, :].rearrange("p l h -> p (l h)"), a["m_s"]).then_inc(small_in, 16)

            def load_half(e):
                n = HALF_OF[e]
                if n >= WRING:
                    old = HALVES_IN_ORDER[n - WRING]
                    last_tile = PASS_TILES[old[1]][-1]
                    if old[0] == "embed" or old[3] == 1:
                        name = ("embed", last_tile, 1) if old[0] == "embed" else (old[0], last_tile, old[2])
                        sp.wait_ge(bank_full[use[name][0]], use[name][1] + 1)
                    else:
                        sp.wait_ge(half_used, sum(f[0] != "embed" and f[3] == 0 for f in HALVES_IN_ORDER[:n - WRING + 1]))
                layer = layer_of(PASS_TILES[e[1]][0])
                sp.dma_start(wring[:, n % WRING].rearrange("p c n -> p (c n)"),
                             a["w"][layer, half_index(e)]).then_inc(half_in[n % WRING], 16)

            loaded = 0
            for e in SCHEDULE:
                if HALF_OF.get(e[:4]) == loaded:
                    load_half(e[:4])
                    loaded += 1
                if e[0] == "layer":
                    layer = e[1]
                    if layer:
                        sp.wait_ge(index_ready, last_chosen(2))
                    sp.dma_start(keys[:, :, :].rearrange("p a b -> p (a b)"), a["keys"][layer]).then_inc(layer_in, 16)
                    sp.dma_start(gain2[:, :], a["gain"][layer]).then_inc(layer_in, 16)
                    sp.dma_start(w_pool[:, :, :].rearrange("p g n -> p (g n)"), a["w_pool"][layer]).then_inc(layer_in, 16)
                if e[0] == "turn" and KIND[e[1]] == "S":
                    layer = layer_of(e[1])
                    sp.wait_ge(index_ready, last_chosen(e[1] - 2))
                    sp.dma_start(scratch[:, :], a["c_s"][layer]).then_inc(states_in, 16)
                    sp.dma_start(pool_buf[:, :], a["pool_buf"][layer]).then_inc(states_in, 16)
                    sp.dma_start(a["out_pool_s"][layer, :, 0:TAIL - 1, :], a["pool_old"][layer, :, 1:TAIL, :]).then_inc(stored, 16)
                if e[0] == "state" and KIND[e[1]] == "B":
                    layer = layer_of(e[1])
                    sp.wait_ge(state_written, count(("state",), e))
                    sp.dma_start(a["out_c_p"][layer], state[:, :, :].rearrange("p h e -> p (h e)")).then_inc(prompt_stored, 16)
                    sp.dma_start(a["out_m_p"][layer:layer + 1, :], m_prev[0:1, :]).then_inc(prompt_stored, 16)
                if e[0] == "sample_write" and e[2] == DEC - 1:
                    layer = layer_of(e[1])
                    sp.wait_ge(sample_state, layer + 1)
                    sp.dma_start(a["out_c_s"][layer], scratch[:, :]).then_inc(samples_stored, 16)
                    sp.dma_start(a["out_m_s"][layer], m_s_new[:, :]).then_inc(samples_stored, 16)
                if e[0] == "pool" and KIND[e[1]] in "BS":
                    layer, kind = layer_of(e[1]), KIND[e[1]]
                    emptied(sp, "project", e[1], 4)
                    if kind == "B":
                        sp.dma_start(a["out_pool_p"][layer], u_in["B"][P - TAIL:P, :]).then_inc(prompt_stored, 16)
                    else:
                        sp.dma_start(a["out_pool_s"][layer, :, TAIL - 1, :], u_in["S"][:, :]).then_inc(samples_stored, 16)
                if e[0] == "gate" and e[2:] == (0, 0, PASS_TILES[e[1]][0]):
                    p, layer = e[1], layer_of(PASS_TILES[e[1]][0])
                    lo, n = ((0, P), (P, P + DEC))[p % 2]
                    if p:
                        b, i = use[("embed", PASS_TILES[p - 1][-1], 1)]
                        sp.wait_ge(bank_full[b], i + 1)
                    sp.dma_start(emb[:, :, 0:n], a["emb"][layer, :, :, lo:lo + n]).then_inc(emb_in, 16)
                if e == ("turn3", 3):
                    sp.wait_ge(index_ready, last_chosen(5))
                    sp.dma_start(gain2[:, :], a["gain"][DEPTH]).then_inc(layer_in, 16)
                if e[0] == "final":
                    kind = KIND[e[1]]
                    sp.wait_ge(x_final, count(("final",), e))
                    lo = {"A": 0, "B": P, "S": SEQ}[kind]
                    sp.dma_start(a["out_y"][lo:lo + ROWS[kind], :], x[kind][:, :]).then_inc(stored, 16)
            sp.wait_ge(stored, 16 * (DEPTH + 3))
            sp.wait_ge(prompt_stored, 48 * DEPTH)
            sp.wait_ge(samples_stored, 48 * DEPTH)

        @block.gpsimd
        def _(pool):
            for t in range(6):
                kind = KIND[t]
                for s in range(SLOTS[kind]):
                    n = FIRST_SLOT[t] + s
                    if s % TOPK == 0:
                        pool.wait_ge(index_ready, chosen_by(t, s // TOPK))
                    if n >= RING:
                        old = n - RING
                        old_tile, old_slot = SLOT_OF[old]
                        if carried(old_tile, old_slot) and old_slot < TOPK - 3:
                            pool.wait_ge(slot_added, VECTOR_ADDED[old] + 1)
                        elif carried(old_tile, old_slot):
                            pool.wait_ge(slot_used, TENSOR_ADDED[old + TOPK - 1 - old_slot])
                        elif TENSOR_ADDED[old] > (TENSOR_ADDED[old - 1] if old else 0):
                            pool.wait_ge(slot_used, TENSOR_ADDED[old])
                        else:
                            pool.wait_ge(slot_added, VECTOR_ADDED[old])
                    pool.indirect_dma_start(
                        out=rows[0:LANES[kind], n % RING, :], out_offset=None, in_=a["uv"],
                        in_offset=bass.IndirectOffsetOnAxis(ap=index[kind][:, s:s + 1], axis=0),
                    ).then_inc(row_in[n % RING], 16)

        @block.scalar
        def _(act):
            after, full, free = reader(act, scalar_step)

            def rms(e, t):
                m, kind, n = rows_of(t), KIND[t], count(RMS_STAGES, e)
                after(act.activation(xn[kind][0:m, :], x[kind][0:m, :], ACT.Square, accum_out=r_in[0:m, :]))
                if n > 1:
                    act.wait_ge(inv_ready, n - 1)
                after(act.activation(r_root[0:m, :], r_in[0:m, :], ACT.Sqrt, scale=1.0 / D, bias=const("eps", m)),
                      root_ready)

            def turn(t):
                if t == 0:
                    act.wait_ge(x_in, 48)
                    act.wait_ge(consts_in, 16)
                if t >= 3:
                    act.wait_ge(x_gated, t - 2)
                rms(("turn", t), t)

            def gates(t):
                m = rows_of(t)
                act.wait_ge(gate_abs, t + 1)
                after(act.activation(gb[0:m, :], ga[0:m, :], ACT.Exp, scale=-1.0))
                after(act.activation(gc[0:m, :], gb[0:m, :], ACT.Ln, bias=1.0), gate_ln)

            def project(p, j, h, t):
                if h == 0:
                    return
                m, kind = rows_of(t), KIND[t]
                if j == 0:
                    act.wait_ge(inv_ready, count(RMS_STAGES, ("turn", t)))
                if (t, j) == (0, 2):
                    act.wait_ge(ones_set, 1)
                if j == 4 and KIND[t] in "BS" and t >= 3:
                    act.wait_ge(prompt_stored if KIND[t] == "B" else samples_stored, 48)
                ps = full("project", t, j)
                scale = inv1[kind][:, 1:2] if j == 1 else inv1[kind][:, 0:1]
                if j == 3:
                    ins = act.activation(o[kind][:, :], ps[0:m, :], ACT.Sigmoid, scale=scale)
                elif j == 2:
                    ins = act.activation(v[kind][:, :, 0:HD], heads_view(ps[0:m, :], m), ACT.Copy, scale=scale)
                else:
                    ins = act.activation({0: q, 1: k, 4: u_in}[j][kind][:, :], ps[0:m, :], ACT.Copy, scale=scale)
                free(ins, "project", t, j)

            def copied(dst, *name):
                free(act.activation(dst, full(*name)[:, :], ACT.Copy), *name)

            def weigh(t):
                act.wait_ge(decay_args, count(("spread",), ("spread", t)))
                for h in range(HEADS):
                    after(act.activation(decayed[:, h, :], decayed[:, h, :], ACT.Exp, bias=neg_m[:, h:h + 1]),
                          *([decay_done] if h == HEADS - 1 else []))
                act.wait_ge(args1_ready, count(("weigh",), ("weigh", t)))
                after(act.activation(exps1[:, 0:8], args1[:, 0:8], ACT.Exp), exps1_ready)

            def turn_qk(t):
                copied(qT[:, :, :].rearrange("p h t -> p (h t)"), "turn_q", t)
                copied(kT[:, :, :].rearrange("p h t -> p (h t)"), "turn_k", t)

            def turn_prod(t):
                copied(decayed[:, :, :].rearrange("p h t -> p (h t)"), "turn_prod", t)

            def values(t):
                if KIND[t] == "B":
                    for i in range(2):
                        ps = full("inter", t, i)
                        for h in range(2):
                            hh = 2 * i + h
                            ins = act.activation(inter[:, hh, :], ps[:, h * 129:h * 129 + 129], ACT.Copy,
                                                 scale=exps1[:, hh:hh + 1])
                            if h == 0:
                                after(ins)
                        free(ins, "inter", t, i)

            def state_args(t):
                act.wait_ge(args2_ready, count(("state",), ("state", t)))
                after(act.activation(exps2[:, :], args2[:, :], ACT.Exp), exps2_ready)

            def sample_read(t):
                act.wait_ge(sample_args, layer_of(t) + 1)
                after(act.activation(exps1[0:DEC, :], args1[0:DEC, :], ACT.Exp), sample_exp)

            def norm_heads(t):
                m = rows_of(t)
                act.wait_ge(head_var, t + 1)
                after(act.activation(h_root[0:m, :], h_in[0:m, :], ACT.Sqrt, scale=1.0 / HD, bias=const("eps", m)),
                      head_root)

            def pool_r(t):
                m = rows_of(t)
                ps = full("pool_r", t)
                free(act.activation(pooled[KIND[t]][:, :, 0:m], heads_view(ps[:, 0:4 * m], m), ACT.Copy), "pool_r", t)

            def turn2(t):
                emptied(act, "mix", t, 0)
                emptied(act, "mix", t, 1)
                rms(("turn2", t), t)

            def query(p, j, h, t):
                if h == 0:
                    return
                m, kind = rows_of(t), KIND[t]
                if j == 0:
                    act.wait_ge(inv_ready, count(RMS_STAGES, ("turn2", t)))
                ps = full("query", t, j)
                free(act.activation(pq[0:m, 1 if kind == "S" else 0, :], ps[0:m, :], ACT.Copy,
                                    scale=inv2[kind][:, 0:1]), "query", t, j)

            def turn_pq(t, j):
                m, kind = rows_of(t), KIND[t]
                ps = full("turn_pq", t, j)
                if kind == "S":
                    act.wait_ge(zeros_set, layer_of(t) + 1)
                    for i in range(4):
                        n = 4 * j + i
                        ins = act.activation(pqT_s[:, n, n * DEC:(n + 1) * DEC], ps[:, i * m:(i + 1) * m], ACT.Copy)
                        if i < 3:
                            after(ins)
                else:
                    ins = act.activation(pqT[:, :, :].rearrange("p h t -> p (h t)"), ps[:, :], ACT.Copy)
                free(ins, "turn_pq", t, j)

            def match_keys(t, j):
                kind = KIND[t]
                if kind == "B" and j == 0:
                    act.wait_ge(samples_stored, 48 * (layer_of(t) + 1))
                if kind != "S":
                    copied(match[:, j * 512:(j + 1) * 512], "match", t, j)
                elif j == 3:
                    ps = full("match", t, j)
                    free(act.activation(match_s, ps[:, 0:P], ACT.Copy), "match", t, j)

            def choose(t, h0, h1):
                m = LANES[KIND[t]]
                act.wait_ge(logits_ready, count(("choose",), ("choose", t, h0, h1)))
                after(act.activation(best[0:m, h0:h1, :], best[0:m, h0:h1, :], ACT.Exp), logits_exp)

            def weights(t, g):
                kind = KIND[t]
                m, lanes, n = ROWS[kind], LANES[kind], FIRST_SLOT[t] // GROUP + g
                act.wait_ge(dot_done, n + 1)
                after(act.activation(gel[0:lanes, n % 4, :], dots[kind][:, g * GROUP:(g + 1) * GROUP],
                                     ACT.Gelu_apprx_tanh), gelu_done)
                act.wait_ge(weight_done, n + 1)
                if n >= DIAGS:
                    act.wait_ge(slot_used, TENSOR_ADDED[(n - DIAGS + 1) * GROUP - 1])
                mine = [i for i in range(GROUP) if on_tensor(t, g * GROUP + i) and not carried(t, g * GROUP + i)]
                for i in mine:
                    own = const("own_token", lanes) if kind == "S" else const("ident")
                    after(act.activation(diag[0:lanes, n % DIAGS, i, 0:m], own, ACT.Copy, scale=wts[0:lanes, n % 4, i:i + 1]),
                          *([diag_done] if i == mine[-1] else []))

            def turn3(t):
                m, n = rows_of(t), 1 if KIND[t] == "S" else 2
                for i in range(n):
                    ps = full("turn3", t, i)
                    c = KT // n
                    free(act.activation(turned[KIND[t]][:, i * c:(i + 1) * c, :],
                                        ps[:, 0:c * m].rearrange("p (h c) -> p h c", h=c), ACT.Copy), "turn3", t, i)

            def gate(p, j, h, t):
                if h == 0:
                    return
                m, kind = rows_of(t), KIND[t]
                ps = full("gate", t, j)
                free(act.activation(xn[kind][0:m, j * BLOCK:(j + 1) * BLOCK], ps[0:m, :], ACT.Sigmoid), "gate", t, j)

            def final(t):
                act.wait_ge(x_gated, t + 1)
                rms(("final", t), t)

            do = {"turn": turn, "gates": gates, "project": project, "weigh": weigh, "turn_qk": turn_qk,
                  "turn_prod": turn_prod, "values": values, "state_args": state_args, "sample_read": sample_read,
                  "norm_heads": norm_heads, "pool_r": pool_r, "turn2": turn2, "query": query, "turn_pq": turn_pq,
                  "match": match_keys, "choose": choose, "turn3": turn3, "gate": gate,
                  "final": final}
            for e in SCHEDULE:
                if e[0] == "slots":
                    weights(*e[1:])
                elif e[0] in do:
                    do[e[0]](*e[1:])

        @block.vector
        def _(dve):
            after, full, free = reader(dve, vector_step)

            def step(ins):
                after(ins)

            def turn_back(name, t, col):
                m, n = rows_of(t), 1 if KIND[t] == "S" else 2
                c = KT // n
                for i in range(n):
                    ps = full(name, t, i)
                    gains = cols[:, layer_of(t), col + i * c:col + (i + 1) * c]
                    free(dve.tensor_tensor(turned[KIND[t]][:, i * c:(i + 1) * c, :],
                                           ps[:, 0:c * m].rearrange("p (h c) -> p h c", h=c), across(gains, m), ALU.mult),
                         name, t, i)

            def invert(e, t, inv):
                m = rows_of(t)
                dve.wait_ge(root_ready, count(RMS_STAGES, e))
                step(dve.reciprocal(inv[:, 0:1], r_root[0:m, :]))
                after(dve.tensor_scalar(inv[:, 1:2], inv[:, 0:1], HD ** -0.5, None, ALU.mult), inv_ready)

            def turn(t):
                if t == 0:
                    dve.wait_ge(small_in, 16 * 4)
                turn_back("turn", t, 0)
                invert(("turn", t), t, inv1[KIND[t]])

            def gates(t):
                m, kind = rows_of(t), KIND[t]
                ps = full("gates", t)
                free(dve.scalar_tensor_tensor(g8[kind][:, :], ps[0:m, 0:8], inv1[kind][:, 0:1],
                                              b_gates[0:m, layer_of(t), :], ALU.mult, ALU.add), "gates", t)
                after(dve.scalar_tensor_tensor(ga[0:m, :], g8[kind][:, 4:8], -1.0, g8[kind][:, 4:8], ALU.mult, ALU.max), gate_abs)
                dve.wait_ge(gate_ln, t + 1)
                after(dve.scalar_tensor_tensor(lf[kind][:, :], g8[kind][:, 4:8], 0.0, gc[0:m, :], ALU.min, ALU.subtract),
                      lf_ready)

            def cumulate(t):
                ps = full("cum", t)
                free(dve.tensor_copy(mb[:, 4:8], ps[:, 0:4]), "cum", t)
                step(dve.tensor_tensor(lead[:, :], g8["A"][:, 0:4], mb[:, 4:8], ALU.subtract))
                after(dve.tensor_tensor(prod[:, :, :], down(const("ident"), HEADS), across(lead[:, :], P), ALU.mult),
                      lead_diag)

            def spread(t):
                ps = full("spread", t)
                free(dve.tensor_tensor(decayed[:, :, :], heads_view(ps[:, :], P), down(const("mask"), HEADS), ALU.add),
                     "spread", t)
                step(dve.tensor_reduce(neg_m[:, :], decayed[:, :, :], AX.X, ALU.max))
                if KIND[t] == "A":
                    step(dve.tensor_scalar(mb[:, 0:4], neg_m[:, :], 0.0, None, ALU.max))
                else:
                    step(dve.tensor_tensor(mb[:, 0:4], neg_m[:, :], m_prev[:, :], ALU.max))
                after(dve.tensor_scalar(neg_m[:, :], mb[:, 0:4], -1.0, None, ALU.mult), decay_args)

            def weigh(t):
                if KIND[t] == "A":
                    step(dve.tensor_copy(args1[:, 0:4], neg_m[:, :]))
                else:
                    step(dve.tensor_tensor(args1[:, 0:4], m_prev[:, :], mb[:, 0:4], ALU.subtract))
                after(dve.tensor_tensor(args1[:, 4:8], neg_m[:, :], mb[:, 4:8], ALU.subtract), args1_ready)

            def scores(t):
                dve.wait_ge(decay_done, count(("weigh",), ("weigh", t)))
                ps = full("scores", t)
                free(dve.tensor_tensor(prod[:, :, :], heads_view(ps[:, :], P), decayed[:, :, :], ALU.mult), "scores", t)

            def values(t):
                if KIND[t] == "B":
                    emptied(dve, "inter", t, 0)
                    emptied(dve, "inter", t, 1)
                for i in range(2):
                    ps = full("values", t, i)
                    two = ps[:, 0:258].rearrange("p (h e) -> p h e", h=2)
                    dst = num[:, 2 * i:2 * i + 2, :]
                    if KIND[t] == "B":
                        ins = dve.tensor_tensor(dst, two, inter[:, 2 * i:2 * i + 2, :], ALU.add)
                    else:
                        ins = dve.tensor_copy(dst, two)
                    free(ins, "values", t, i)

            def state_args(t):
                kind = KIND[t]
                ps = full("last", t)
                free(dve.tensor_copy(last[:, :], ps[:, 0:8]), "last", t)
                step(dve.tensor_tensor(args2[:, 0:4], lead[:, :], last[:, 0:4], ALU.subtract))
                if kind == "A":
                    if t:
                        dve.wait_ge(prompt_stored, 48)
                    after(dve.tensor_scalar(args2[:, 4:8], last[:, 0:4], -1.0, None, ALU.mult), args2_ready)
                else:
                    after(dve.tensor_tensor(args2[:, 4:8], m_prev[:, :], last[:, 0:4], ALU.subtract), args2_ready)
                step(dve.tensor_tensor(m_prev[:, :], last[:, 0:4], last[:, 4:8], ALU.add))

            def weigh_keys(t):
                dve.wait_ge(exps2_ready, count(("state",), ("state", t)))
                emptied(dve, "project", t, 1)
                after(dve.tensor_tensor(prod[:, :, :], heads_view(k["A"][:, :], P), across(exps2[:, 0:4], P), ALU.mult),
                      k_weighted)

            def state_update(t):
                kind = KIND[t]
                for i in range(2):
                    ps = full("state", t, i)
                    if kind == "A":
                        ins = dve.tensor_copy(state[:, 2 * i:2 * i + 2, :], ps[:, 0:258].rearrange("p (h e) -> p h e", h=2))
                    else:
                        for h in range(2):
                            hh = 2 * i + h
                            ins = dve.scalar_tensor_tensor(state[:, hh, :], state[:, hh, :], exps2[:, 4 + hh:5 + hh],
                                                           ps[:, h * 129:h * 129 + 129], ALU.mult, ALU.add)
                            if h == 0:
                                step(ins)
                    free(ins, "state", t, i)
                after(dve.tensor_copy(den[0:1, 0:1], state[0:1, 0, 0:1]), state_written)

            def sample_read(t):
                n, layer = layer_of(t) + 1, layer_of(t)
                ig = g8["S"][:, 0:4]
                if layer:
                    dve.wait_ge(samples_stored, 48)
                step(dve.tensor_tensor(args1[0:DEC, 0:4], lf["S"][:, :], m_s[:, layer, :], ALU.add))
                step(dve.tensor_tensor(m_s_new[:, :], ig, args1[0:DEC, 0:4], ALU.max))
                step(dve.tensor_tensor(args1[0:DEC, 0:4], args1[0:DEC, 0:4], m_s_new[:, :], ALU.subtract))
                step(dve.tensor_tensor(args1[0:DEC, 4:8], ig, m_s_new[:, :], ALU.subtract))
                after(dve.tensor_scalar(args1[0:DEC, 8:12], m_s_new[:, :], -1.0, None, ALU.mult), sample_args)
                ps = full("turn_qs", t)
                free(dve.tensor_tensor(
                    q_own[:, :, :, :],
                    ps[:, 0:32].rearrange("p (h b o) -> p h b o", h=HEADS, o=1).to_broadcast([P, HEADS, DEC, DEC]),
                    const("own").rearrange("p (o b j) -> p o b j", o=1, b=DEC).to_broadcast([P, HEADS, DEC, DEC]),
                    ALU.mult), "turn_qs", t)
                dve.wait_ge(sample_exp, n)
                after(dve.tensor_tensor(w_own[:, :, :], const("own_head", DEC).rearrange("p (b h) -> p b h", b=DEC),
                                        down(exps1[0:DEC, 0:4], DEC), ALU.mult), w_own_ready)
                emptied(dve, "project", t, 0)
                emptied(dve, "project", t, 1)
                emptied(dve, "project", t, 2)
                s512 = junk[0:DEC, :, :]
                step(dve.tensor_tensor(s512, heads_view(q["S"][:, :], DEC), heads_view(k["S"][:, :], DEC), ALU.mult))
                step(dve.tensor_reduce(qk_s[:, :], s512, AX.X, ALU.add))
                step(dve.tensor_tensor(qk_s[:, :], qk_s[:, :], exps1[0:DEC, 4:8], ALU.mult))
                step(dve.tensor_tensor(inter[0:DEC, :, :], v["S"][:, :, :], across(qk_s[:, :], HD + 1), ALU.mult))
                step(dve.tensor_tensor(heads_view(k["S"][:, :], DEC), heads_view(k["S"][:, :], DEC),
                                       across(exps1[0:DEC, 4:8], HD), ALU.mult))
                ps = full("w_spread", t)
                free(dve.tensor_copy(w_spread[:, :], ps[:, 0:32]), "w_spread", t)
                for i in range(2):
                    ps = full("read", t, i)
                    for h in range(2):
                        hh = 2 * i + h
                        ins = dve.scalar_tensor_tensor(num[0:DEC, hh, :], ps[0:DEC, h * 129:h * 129 + 129],
                                                       exps1[0:DEC, hh:hh + 1], inter[0:DEC, hh, :], ALU.mult, ALU.add)
                        if h == 0:
                            step(ins)
                    free(ins, "read", t, i)

            def sample_k_own(t, b):
                after(dve.tensor_scalar(pq[0:DEC, b % 2, :], k["S"][:, :], const("ident", DEC)[:, b:b + 1], None, ALU.mult),
                      sample_k)

            def sample_write(t, b):
                if b == 0:
                    sample_k_own(t, 0)
                if b + 1 < DEC:
                    sample_k_own(t, b + 1)
                for i in range(2):
                    ps = full("write", t, b, i)
                    for h in range(2):
                        s = b * HEADS + 2 * i + h
                        ins = dve.scalar_tensor_tensor(cs[:, s, :], cs[:, s, :], w_spread[:, s:s + 1],
                                                       ps[:, h * 129:h * 129 + 129], ALU.mult, ALU.add)
                        if h == 0:
                            step(ins)
                    free(ins, "write", t, b, i)
                if b == DEC - 1:
                    after(dve.tensor_copy(den[0:1, 0:1], cs[0:1, 0, 0:1]), sample_state)

            def norm_heads(t):
                m, kind = rows_of(t), KIND[t]
                if kind == "S":
                    floor = exps1[0:m, 8:12]
                else:
                    dve.wait_ge(exps1_ready, count(("weigh",), ("weigh", t)))
                    floor = exps1[:, 4:8]
                n3 = num[0:m, :, 0:HD]
                o3 = heads_view(o[kind][:, :], m)
                total = num[0:m, :, HD:HD + 1].rearrange("p h o -> p (h o)")
                step(dve.scalar_tensor_tensor(den[0:m, :], total, -1.0, total, ALU.mult, ALU.max))
                step(dve.tensor_tensor(den[0:m, :], den[0:m, :], floor, ALU.max))
                step(dve.reciprocal(den[0:m, :], den[0:m, :]))
                step(dve.tensor_tensor(n3, n3, across(den[0:m, :], HD), ALU.mult))
                step(dve.tensor_tensor(junk[0:m, :, :], n3, n3, ALU.mult))
                after(dve.tensor_reduce(h_in[0:m, :], junk[0:m, :, :], AX.X, ALU.add), head_var)
                emptied(dve, "project", t, 3)
                step(dve.tensor_tensor(n3, n3, o3, ALU.mult))
                dve.wait_ge(head_root, t + 1)
                step(dve.reciprocal(h_inv[0:m, :], h_root[0:m, :]))
                after(dve.tensor_tensor(n3, n3, across(h_inv[0:m, :], HD), ALU.mult), heads_ready)

            def heads(t):
                m, kind = rows_of(t), KIND[t]
                ps = full("heads", t)
                free(dve.tensor_tensor(turned[kind][:, 0:4, :], heads_view(ps[:, 0:4 * m], m),
                                       across(cols[:, layer_of(t), 16:20], m), ALU.mult), "heads", t)

            def pool(t):
                m = rows_of(t)
                ps = full("pool_z", t)
                free(dve.tensor_tensor(turned[KIND[t]][:, 4:8, :], heads_view(ps[:, 0:4 * m], m),
                                       across(cols[:, layer_of(t), 20:24], m), ALU.mult), "pool_z", t)

            def mix(p, j, h, t):
                if h == 0:
                    return
                m = rows_of(t)
                part = x[KIND[t]][:, j * BLOCK:(j + 1) * BLOCK]
                free(dve.tensor_tensor(part, part, full("mix", t, j)[0:m, :], ALU.add), "mix", t, j)

            def turn2(t):
                kind = KIND[t]
                turn_back("turn2", t, 8)
                invert(("turn2", t), t, inv2[kind])
                dve.wait_ge(layer_in, 48 * (layer_of(t) + 1))
                if kind != "S":
                    step(dve.scalar_tensor_tensor(xn[kind][:, :], x[kind][:, :], inv2[kind][:, 0:1], gain2[:, :],
                                                  ALU.mult, ALU.mult))
                    return
                after(dve.memset(pqT_s, 0.0), zeros_set)
                ps = full("rep_inv", t)
                free(dve.tensor_copy(inv_rep[:, :], ps[0:64, 0:1]), "rep_inv", t)
                for i in range(2):
                    lo = i * BLOCK
                    ps = full("rep", t, i)
                    free(dve.scalar_tensor_tensor(xn[kind][:, lo:lo + BLOCK], ps[0:64, :], inv_rep[:, 0:1],
                                                  gain2[0:64, lo:lo + BLOCK], ALU.mult, ALU.mult), "rep", t, i)

            def top16(values, idx, src):
                step(dve.max(values[:, 0:8], src))
                step(dve.max_index(idx[:, 0:8], values[:, 0:8], src))
                step(dve.match_replace(src, values[:, 0:8], src, REMOVED))
                step(dve.max(values[:, 8:16], src))
                step(dve.max_index(idx[:, 8:16], values[:, 8:16], src))

            def rank(t, i):
                if KIND[t] == "S":
                    emptied(dve, "match", t, 3)
                    top16(top[:, 0, :], top_i[:, 0, :], match_s)
                    return
                emptied(dve, "match", t, i // 4)
                top16(top[:, i, :], top_i[:, i, :], match[:, i * P:(i + 1) * P])

            def pairs(t, h0, h1):
                kind, first = KIND[t], float(layer_of(t) * EXPERTS)
                if kind == "S":
                    m, hs = PH * DEC, 1
                    after(dve.tensor_copy(top_f[:, 0, :], top_i[:, 0, :]), pair_src)
                    ps = full("pairs", t)
                    free(dve.tensor_copy(pair_s[:, :, :], ps[0:64, 0:64].rearrange("p (c k) -> p c k", c=4)), "pairs", t)
                    v0, i0, v1, i1 = (pair_s[:, c:c + 1, :] for c in range(4))
                else:
                    m, hs = P, h1 - h0
                    mine = slice(2 * h0, 2 * h1)
                    step(dve.tensor_copy(top_f[:, mine, :], top_i[:, mine, :]))
                    vals = top[:, mine, :].rearrange("p (h c) k -> p h c k", c=2)
                    inds = top_f[:, mine, :].rearrange("p (h c) k -> p h c k", c=2)
                    v0, v1, i0, i1 = vals[:, :, 0, :], vals[:, :, 1, :], inds[:, :, 0, :], inds[:, :, 1, :]
                b0 = base[0:m, h0:h1, :]
                step(dve.tensor_scalar(b0, i0, float(NKEYS), first, ALU.mult, ALU.add))
                for dst, s0, s1 in ((sums, v0, v1), (codes, b0, i1)):
                    at = 0
                    for r in range(TOPK // 2):
                        n = STAIR[r]
                        dve.tensor_tensor(dst[0:m, h0:h1, at:at + n], s0[:, :, r:r + 1].to_broadcast([m, hs, n]),
                                          s1[:, :, 0:n], ALU.add)
                        at += n
                    n = TOPK // 2
                    step(dve.tensor_tensor(dst[0:m, h0:h1, at:at + n], s0[:, :, n:2 * n],
                                           s1[:, :, 0:1].to_broadcast([m, hs, n]), ALU.add))

            def find_best(t, h):
                m = LANES[KIND[t]]
                top16(best[0:m, h, :], best_i[0:m, h, :], sums[0:m, h, :])
                step(dve.tensor_copy(best_f[0:m, h, :], best_i[0:m, h, :]))
                shape = [m, TOPK, CANDS]
                hot = onehot[0:m, :, :]
                step(dve.tensor_tensor(hot, down(const("place", m), TOPK), across(best_f[0:m, h, :], CANDS), ALU.is_equal))
                step(dve.tensor_tensor(hot, hot, down(codes[0:m, h, :], TOPK), ALU.mult))
                step(dve.tensor_reduce(chosen[0:m, h, :], hot, AX.X, ALU.add))

            def choose(t, h0, h1):
                kind = KIND[t]
                m, n = LANES[kind], h1 - h0
                turn_no = count(("choose",), ("choose", t, h0, h1))
                mine = slice(h0 * TOPK, h1 * TOPK)
                scored, largest, share = best[0:m, h0:h1, :], base[0:m, h0:h1, 0:1], shares[0:m, h0:h1]
                step(dve.tensor_copy(largest, best[0:m, h0:h1, 0:1]))
                after(dve.tensor_tensor(scored, scored, largest.to_broadcast([m, n, TOPK]), ALU.subtract), logits_ready)
                dve.wait_ge(logits_exp, turn_no)
                step(dve.tensor_reduce(share, scored, AX.X, ALU.add))
                step(dve.reciprocal(share, share))
                step(dve.tensor_tensor(prob[kind][:, mine].rearrange("p (h k) -> p h k", h=n), scored,
                                       across(share, TOPK), ALU.mult))
                after(dve.tensor_copy(index[kind][:, mine].rearrange("p (h k) -> p h k", h=n), chosen[0:m, h0:h1, :]),
                      index_ready)

            def take_dots(t, g):
                kind = KIND[t]
                lanes = LANES[kind]
                for i in range(GROUP):
                    n = FIRST_SLOT[t] + g * GROUP + i
                    dve.wait_ge(row_in[n % RING], 16 * (n // RING + 1))
                    u = rows[0:lanes, n % RING, 0:D]
                    s = g * GROUP + i
                    ins = dve.scalar_tensor_tensor(u, u, 1.0, xn[kind][:, :], ALU.mult, ALU.mult,
                                                   accum_out=dots[kind][:, s:s + 1])
                ins.then_inc(dot_done, 1)

            def weights(t, g):
                lanes, n = LANES[KIND[t]], FIRST_SLOT[t] // GROUP + g
                dve.wait_ge(gelu_done, n + 1)
                after(dve.tensor_tensor(wts[0:lanes, n % 4, :], gel[0:lanes, n % 4, :],
                                        prob[KIND[t]][:, g * GROUP:(g + 1) * GROUP], ALU.mult), weight_done)

            def add_own_values(t, g):
                lanes, n = LANES[KIND[t]], FIRST_SLOT[t] // GROUP + g
                for i in range(GROUP):
                    s, at = g * GROUP + i, n * GROUP + i
                    if carried(t, s):
                        v_row, weight = rows[0:lanes, at % RING, D:2 * D], wts[0:lanes, n % 4, i:i + 1]
                        if s == 1:
                            ins = dve.tensor_scalar(v_row, v_row, weight, None, ALU.mult)
                        else:
                            ins = dve.scalar_tensor_tensor(v_row, v_row, weight, rows[0:lanes, (at - 2) % RING, D:2 * D],
                                                           ALU.mult, ALU.add)
                        after(ins, carry_done if s == TOPK - 1 else slot_added)
                    elif not on_tensor(t, s):
                        v_row = rows[0:lanes, (n * GROUP + i) % RING, D:2 * D]
                        after(dve.scalar_tensor_tensor(x[KIND[t]][:, :], v_row, wts[0:lanes, n % 4, i:i + 1],
                                                       x[KIND[t]][:, :], ALU.mult, ALU.add), slot_added)

            def add_experts(t):
                kind = KIND[t]
                m = ROWS[kind]
                dve.wait_ge(slot_used, TENSOR_ADDED[FIRST_SLOT[t] + SLOTS[kind] - 1])
                after(dve.tensor_tensor(x[kind][:, :], x[kind][:, :], acc[0:m, :, :].rearrange("p c n -> p (c n)"), ALU.add),
                      acc_read)

            def embed(p):
                for t in PASS_TILES[p]:
                    m, kind = rows_of(t), KIND[t]
                    for j in range(2):
                        emptied(dve, "gate", t, j)
                        ps = full("embed", t, j)
                        sig = xn[kind][0:m, j * BLOCK:(j + 1) * BLOCK]
                        free(dve.tensor_tensor(sig, sig, ps[0:m, :], ALU.mult), "embed", t, j)
                    after(dve.tensor_tensor(x[kind][:, :], x[kind][:, :], xn[kind][0:m, :], ALU.add), x_gated)

            def final(t):
                kind = KIND[t]
                invert(("final", t), t, inv2[kind])
                dve.wait_ge(layer_in, 16 * (3 * DEPTH + 1))
                after(dve.scalar_tensor_tensor(x[kind][:, :], x[kind][:, :], inv2[kind][:, 0:1], gain2[0:rows_of(t), :],
                                               ALU.mult, ALU.mult), x_final)

            dve.memset(v["A"][:, :, HD:HD + 1], 1.0)
            after(dve.memset(v["S"][:, :, HD:HD + 1], 1.0), ones_set)

            do = {"turn": turn, "gates": gates, "cum": cumulate, "spread": spread, "weigh": weigh, "scores": scores,
                  "values": values, "state_args": state_args, "weigh_keys": weigh_keys, "state": state_update,
                  "sample_read": sample_read, "sample_write": sample_write, "norm_heads": norm_heads, "heads": heads, "pool": pool, "mix": mix, "turn2": turn2, "rank": rank, "pairs": pairs,
                  "best": find_best, "choose": choose, "embed": embed, "final": final}
            late = older = None
            for e in SCHEDULE:
                if e[0] in ("slots", "flush"):
                    if e[0] == "slots":
                        take_dots(*e[1:])
                    if late:
                        add_own_values(*late)
                    if e[0] == "slots":
                        weights(*e[1:])
                    if older and older[1] == SLOTS[KIND[older[0]]] // GROUP - 1:
                        add_experts(older[0])
                    older, late = late, e[1:]
                    if e[0] == "flush":
                        add_experts(older[0])
                elif e[0] in do:
                    do[e[0]](*e[1:])


def shape_constants():
    c = {n: np.zeros((P, w), np.float32) for n, w in _widths}
    r = np.arange(P)
    c["ident"][:] = np.eye(P)
    c["tri"][:] = r[:, None] <= r[None, :]
    c["mask"][:] = np.where(r[None, :] <= r[:, None], 0.0, NEG)
    c["ones"][:] = 1.0
    for g, w in enumerate(WINDOWS):
        s, t = r[:, None], r[None, :]
        inside = (s <= t) & (s > t - w)
        cols = slice(g * P, (g + 1) * P)
        c["band_a"][:, cols] = inside / np.minimum(t + 1, w) - np.eye(P)
        c["band_b"][:, cols] = inside / w - np.eye(P)
        c["band_prev"][:, cols] = ((s - P > t - w)) / w
        for b in range(DEC):
            c["band_buf"][b * TAIL + TAIL - (w - 1):(b + 1) * TAIL, g * 8 + b] = 1.0 / w
            c["band_new"][b, g * 8 + b] = 1.0 / w - 1.0
    for b in range(DEC):
        c["own"][:, b * DEC + b] = 1.0
        c["own_head"][b, b * HEADS:(b + 1) * HEADS] = 1.0
        for h in range(PH):
            for half in range(2):
                c[f"key{half}"][(2 * h + half) * DEC + b, h * DEC + b] = 1.0
            c["copy8"][b, h * DEC + b] = 1.0
            c["own_token"][h * DEC + b, b] = 1.0
    c["place"][:] = np.arange(CANDS)
    c["eps"][:] = EPS
    return np.concatenate([c[n] for n, _ in _widths], axis=1)


OUTS = {"out_y": (SEQ + DEC, D), "out_c_p": (DEPTH, P, HEADS * (HD + 1)), "out_m_p": (DEPTH, HEADS),
        "out_pool_p": (DEPTH, TAIL, POOLW), "out_c_s": (DEPTH, P, DEC * HEADS * (HD + 1)),
        "out_m_s": (DEPTH, DEC, HEADS), "out_pool_s": (DEPTH, DEC, TAIL, POOLW)}


def layout(i):
    f = {n: np.asarray(z) for n, z in i.items()}

    def halves(w):
        n = w.shape[2] // BLOCK
        return w.reshape(DEPTH, 2, 4, P, n, BLOCK).transpose(0, 4, 1, 3, 2, 5).reshape(DEPTH, 2 * n, P, 4 * BLOCK)

    w_in = f["w_in"]
    dense_in, gates_in = w_in[:, :, :2560], w_in[:, :, 2560:]
    ple = f["w_ple"].reshape(DEPTH, 1, 2, P, 2, BLOCK).transpose(0, 1, 3, 4, 2, 5).reshape(DEPTH, 1, P, 4 * BLOCK)
    emb = np.concatenate([f["p_prompt"][:, 0], f["p_sample"][:, :, 0]], axis=1)

    def column(name, n):
        return f[name].reshape(DEPTH, n, P).transpose(2, 0, 1)

    c_n = np.concatenate([f["state_C"], f["state_n"][..., None]], axis=-1)
    return {
        "x": np.concatenate([f["x_prompt"][0], f["x_sample"][:, 0]], axis=0),
        "consts": shape_constants(),
        "w": np.concatenate([halves(dense_in), halves(f["w_out"]), halves(f["peer_wq"]), halves(f["w_gate"]), ple], axis=1),
        "w_gates": gates_in.reshape(DEPTH, KT, P, 8).transpose(2, 0, 1, 3).reshape(P, -1),
        "b_gates": np.broadcast_to(f["b_gate"].reshape(1, -1), (P, DEPTH * 8)),
        "cols": np.concatenate([column("norm1", 8), column("norm2", 8), column("mlstm_norm", 4), column("pool_scale", 4)],
                               axis=2).reshape(P, -1),
        "w_pool": f["w_pool"].transpose(0, 2, 1, 3).reshape(DEPTH, P, -1),
        "emb": emb.reshape(DEPTH, SEQ + DEC, 2, P).transpose(0, 3, 2, 1),
        "m_s": f["state_m"].transpose(1, 0, 2).reshape(DEC, -1),
        "keys": f["peer_keys"].transpose(0, 4, 2, 1, 3).reshape(DEPTH, P, -1),
        "gain": np.broadcast_to(np.concatenate([f["norm2"], f["norm_f"][None]])[:, None], (DEPTH + 1, P, D)),
        "c_s": c_n.transpose(0, 3, 1, 2, 4).reshape(DEPTH, P, -1),
        "pool_buf": f["state_pool"].reshape(DEPTH, DEC * TAIL, POOLW),
        "pool_old": f["state_pool"],
        "uv": np.concatenate([f["peer_u"], f["peer_v"]], axis=2).reshape(DEPTH * EXPERTS, 2 * D),
    }


def kernel(**inputs):
    import concourse.bacc as bacc
    from concourse.bass_utils import run_bass_kernel_spmd

    nc = bacc.Bacc("TRN2", target_bir_lowering=False, num_devices=1)
    arrays, a = {}, {}
    for name, z in layout(inputs).items():
        arrays[f"in_{name}"] = np.ascontiguousarray(z)
        a[name] = nc.dram_tensor(f"in_{name}", z.shape, F32, kind="ExternalInput").ap()
    for name, shape in OUTS.items():
        a[name] = nc.dram_tensor(name, shape, F32, kind="ExternalOutput").ap()
    build(nc, a)
    r = run_bass_kernel_spmd(nc, [arrays], core_ids=[0]).results[0]
    y = r["out_y"]
    c_p = r["out_c_p"].reshape(DEPTH, HD, 1, HEADS, HD + 1).transpose(0, 2, 3, 1, 4)
    c_s = r["out_c_s"].reshape(DEPTH, HD, DEC, HEADS, HD + 1).transpose(0, 2, 3, 1, 4)
    return (y[:SEQ].reshape(1, SEQ, D), y[SEQ:].reshape(DEC, 1, D),
            np.ascontiguousarray(c_p[..., :HD]), np.ascontiguousarray(c_p[..., HD]),
            r["out_m_p"].reshape(DEPTH, 1, HEADS), r["out_pool_p"].reshape(DEPTH, 1, TAIL, POOLW),
            np.ascontiguousarray(c_s[..., :HD]), np.ascontiguousarray(c_s[..., HD]),
            r["out_m_s"], r["out_pool_s"])
```
